# Optimizing a Trainium2 kernel written in Bass

```python
import math, functools
import jax, jax.numpy as jnp
from jax import lax
import numpy as np

D_MODEL = 1024
BATCH = 1
SEQ = 1024
DEPTH = 1

N_META = 16
MIX_WIDTH = D_MODEL
MIX_A = MIX_WIDTH // 2
MIX_B = MIX_WIDTH - MIX_A
N_POOL_GROUPS = 4
POOL_GROUP_DIM = MIX_A // N_POOL_GROUPS
POOL_WINDOWS = (2, 4, 8, 16)
N_CONV_HEADS = 8
CONV_WIDTH = 3
MIX_IN = MIX_A + 3 * MIX_B
N_PEER_HEADS = 8
N_KEYS = 128
N_EXPERTS = N_KEYS * N_KEYS
D_QUERY = 256
D_QUERY_HALF = D_QUERY // 2
PEER_TOPK = 16
TOKEN_BLOCK = 128
EPS = 1e-6

kernel_name = "hymba_pool_shortconv_peer_layer"

def rmsnorm(x, g):
    xf = x.astype(jnp.float32)
    y = xf * lax.rsqrt(jnp.mean(xf * xf, axis=-1, keepdims=True) + EPS)
    return (y * g.astype(jnp.float32)).astype(x.dtype)

def causal_pool_minus_self(u, window):
    L = u.shape[1]
    uf = u.astype(jnp.float32)
    c = jnp.cumsum(uf, axis=1)
    c_shift = jnp.pad(c, ((0, 0), (window, 0), (0, 0)))[:, :L]
    count = jnp.minimum(jnp.arange(1, L + 1), window).astype(jnp.float32)
    mean = (c - c_shift) / count[None, :, None]
    return (mean - uf).astype(u.dtype)

def pool_mixer(a, pool_w, pool_scale):
    B, L, _ = a.shape
    groups = a.reshape(B, L, N_POOL_GROUPS, POOL_GROUP_DIM)
    pooled = jnp.stack([causal_pool_minus_self(groups[:, :, g], POOL_WINDOWS[g])
                        for g in range(N_POOL_GROUPS)], axis=2)
    y = jnp.einsum('blgc,gcd->blgd', pooled, pool_w)
    return y.reshape(B, L, MIX_A) * pool_scale

def short_conv_mixer(b_gate, c_gate, val, conv_w):
    u = c_gate * val
    L = u.shape[1]
    up = jnp.pad(u, ((0, 0), (CONV_WIDTH - 1, 0), (0, 0)))
    conv = up[:, 0:L] * conv_w[0]
    for k in range(1, CONV_WIDTH):
        conv = conv + up[:, k:k + L] * conv_w[k]
    return b_gate * conv

def peer_retrieve(xn, w_query, sub_keys):
    T = xn.shape[0]
    q = (xn @ w_query).reshape(T, N_PEER_HEADS, 2, D_QUERY_HALF)
    s = jnp.einsum('thpc,hpkc->thpk', q.astype(jnp.float32), sub_keys.astype(jnp.float32))
    s1, i1 = lax.top_k(s[:, :, 0], PEER_TOPK)
    s2, i2 = lax.top_k(s[:, :, 1], PEER_TOPK)
    cand_s = (s1[..., :, None] + s2[..., None, :]).reshape(T, N_PEER_HEADS, PEER_TOPK * PEER_TOPK)
    cand_i = (i1[..., :, None] * N_KEYS + i2[..., None, :]).reshape(T, N_PEER_HEADS, PEER_TOPK * PEER_TOPK)
    top_s, pos = lax.top_k(cand_s, PEER_TOPK)
    idx = jnp.take_along_axis(cand_i, pos, axis=-1)
    gates = jax.nn.softmax(top_s, axis=-1)
    return idx, gates

def peer_experts(xn, idx, gates, expert_u, expert_v):
    T, D = xn.shape
    HK = N_PEER_HEADS * PEER_TOPK
    pad = (-T) % TOKEN_BLOCK
    xb = jnp.pad(xn, ((0, pad), (0, 0))).reshape(-1, TOKEN_BLOCK, D)
    ib = jnp.pad(idx.reshape(T, HK), ((0, pad), (0, 0))).reshape(-1, TOKEN_BLOCK, HK)
    gb = jnp.pad(gates.reshape(T, HK), ((0, pad), (0, 0))).reshape(-1, TOKEN_BLOCK, HK)

    def block(args):
        xblk, iblk, gblk = args
        u = expert_u[iblk]
        v = expert_v[iblk]
        act = jax.nn.gelu(jnp.einsum('tkd,td->tk', u, xblk).astype(jnp.float32), approximate=False)
        return jnp.einsum('tk,tkd->td', (gblk * act).astype(v.dtype), v)

    out = lax.map(block, (xb, ib, gb))
    return out.reshape(-1, D)[:T].astype(xn.dtype)

def setup_inputs(seed: int = 0) -> dict:
    key = jax.random.key(seed)
    ks = jax.random.split(key, 16)
    f32 = jnp.float32
    nrm = lambda k, shape, scale: jax.random.normal(k, shape, f32) * scale
    gain = lambda k, shape: 1.0 + 0.02 * jax.random.normal(k, shape, f32)
    return {
        "x": jax.random.normal(ks[0], (BATCH, SEQ, D_MODEL), f32),
        "meta_tokens": nrm(ks[1], (N_META, D_MODEL), 1.0),
        "norm_mix_g": gain(ks[2], (DEPTH, D_MODEL)),
        "w_in": nrm(ks[3], (DEPTH, D_MODEL, MIX_IN), D_MODEL ** -0.5),
        "pool_w": nrm(ks[4], (DEPTH, N_POOL_GROUPS, POOL_GROUP_DIM, POOL_GROUP_DIM), POOL_GROUP_DIM ** -0.5),
        "pool_scale": 1.0 + 0.1 * jax.random.normal(ks[5], (DEPTH, MIX_A), f32),
        "conv_w": nrm(ks[6], (DEPTH, CONV_WIDTH, MIX_B), CONV_WIDTH ** -0.5),
        "norm_a_g": gain(ks[7], (DEPTH, MIX_A)),
        "norm_b_g": gain(ks[8], (DEPTH, MIX_B)),
        "w_out": nrm(ks[9], (DEPTH, MIX_WIDTH, D_MODEL), MIX_WIDTH ** -0.5),
        "norm_ffn_g": gain(ks[10], (DEPTH, D_MODEL)),
        "w_query": nrm(ks[11], (DEPTH, D_MODEL, N_PEER_HEADS * D_QUERY), D_MODEL ** -0.5),
        "sub_keys": nrm(ks[12], (DEPTH, N_PEER_HEADS, 2, N_KEYS, D_QUERY_HALF), D_QUERY_HALF ** -0.5),
        "expert_u": nrm(ks[13], (DEPTH, N_EXPERTS, D_MODEL), D_MODEL ** -0.5),
        "expert_v": nrm(ks[14], (DEPTH, N_EXPERTS, D_MODEL), 0.5),
        "norm_final_g": gain(ks[15], (D_MODEL,)),
    }

def reference(x, meta_tokens, norm_mix_g, w_in, pool_w, pool_scale, conv_w, norm_a_g, norm_b_g,
              w_out, norm_ffn_g, w_query, sub_keys, expert_u, expert_v, norm_final_g):
    B = x.shape[0]
    meta = jnp.broadcast_to(meta_tokens.astype(x.dtype)[None], (B, N_META, D_MODEL))
    h = jnp.concatenate([meta, x], axis=1)
    for layer in range(DEPTH):
        xn = rmsnorm(h, norm_mix_g[layer])
        proj = xn @ w_in[layer]
        a = proj[..., :MIX_A]
        b_gate = proj[..., MIX_A:MIX_A + MIX_B]
        c_gate = proj[..., MIX_A + MIX_B:MIX_A + 2 * MIX_B]
        val = proj[..., MIX_A + 2 * MIX_B:]
        ya = rmsnorm(pool_mixer(a, pool_w[layer], pool_scale[layer]), norm_a_g[layer])
        yb = rmsnorm(short_conv_mixer(b_gate, c_gate, val, conv_w[layer]), norm_b_g[layer])
        h = h + jnp.concatenate([ya, yb], axis=-1) @ w_out[layer]
        if layer == DEPTH - 1:
            h = h[:, N_META:]
        Bh, Lh, _ = h.shape
        xf = rmsnorm(h, norm_ffn_g[layer]).reshape(Bh * Lh, D_MODEL)
        idx, gates = peer_retrieve(xf, w_query[layer], sub_keys[layer])
        h = h + peer_experts(xf, idx, gates, expert_u[layer], expert_v[layer]).reshape(Bh, Lh, D_MODEL)
    return rmsnorm(h, norm_final_g)


_drawn_inputs = setup_inputs


def setup_inputs(seed=0):
    import zlib

    import numpy as np

    out = dict(_drawn_inputs(seed))
    spreads = {}
    factors = {'meta_tokens': 2.734,
     'norm_a_g': 30.076,
     'norm_b_g': 31.472,
     'norm_final_g': 23.553,
     'norm_ffn_g': 16.868}
    for name, (base, spread) in spreads.items():
        noise = np.random.default_rng([zlib.crc32(name.encode()), seed]).standard_normal(out[name].shape)
        drawn = base * np.exp(spread * noise) if base else spread * noise
        out[name] = __import__('jax').numpy.asarray(drawn.astype(out[name].dtype))
    for name, factor in factors.items():
        out[name] = (out[name] * factor).astype(out[name].dtype)
    return out
```

```python
import concourse.bass as bass
from concourse import mybir
from concourse.alu_op_type import AluOpType as ALU
from contextlib import ExitStack

FP32 = mybir.dt.float32
U32 = mybir.dt.uint32
ACT = mybir.ActivationFunctionType
AX = mybir.AxisListType

P = 128
D = 1024
KD = D // P
SEQ, META = 1024, 16
HALVES = 2
HT = SEQ // HALVES
TT = HT // P
TILES = SEQ // P
COLS = HT + META
HB = COLS // 2
CT = 16
NG = 4
HEADS, KEYS, TOPK = 8, 128, 16
HP = 2 * HEADS
HK = HEADS * TOPK
SLOTW = 512
EPS = 1e-6
LOWEST = -3.0e38
RING = 16
CREDIT = RING


def program(nc, hT, x, w_in, w_out, w_query, sub_keys, pool_w, small, rows_g, expert_u, expert_v, out):
    h2_d = nc.dram_tensor("h2_scratch", (TILES, P, D), FP32, kind="Internal").ap()
    xf_d = nc.dram_tensor("xf_scratch", (TILES, P, D), FP32, kind="Internal").ap()
    s_d = nc.dram_tensor("score_scratch", (TILES, P, HP * KEYS), FP32, kind="Internal").ap()

    steps = ([("sumsq", 0, "act")] + [("proj", c, "act") for c in range(CT)]
             + [("pool", i, "act") for i in range(2)] + [("ynorm", 0, "act")]
             + [("outp", t, "dve") for t in range(TT)] + [("turn", t, "act") for t in range(TT)]
             + [("query", c, "act") for c in range(CT // 2)] + [("score", i, "act") for i in range(2 * TT)])
    NSTEP = len(steps)
    PAIRS = 4
    assert NSTEP % PAIRS == 0
    position = {(kind, i): n for n, (kind, i, _) in enumerate(steps)}
    per_half = {e: sum(s[2] == e for s in steps) for e in ("act", "dve")}

    def emptied_until(n):
        e = steps[n][2]
        return e, sum(s[2] == e for s in steps[:n + 1])

    LOADS = 10

    ctx = ExitStack()
    with ctx:
        def sb(name, shape, dt=FP32):
            return ctx.enter_context(nc.sbuf_tensor(name, shape, dt))

        def sem(name):
            return ctx.enter_context(nc.semaphore(name))

        arena = sb("arena", [P, 2 * KD * SLOTW + KD * HT + KD * COLS])
        wslot = [arena[:, i * KD * SLOTW:(i + 1) * KD * SLOTW].rearrange("p (k n) -> p k n", k=KD) for i in range(2)]
        o = 2 * KD * SLOTW
        yT = arena[:, o:o + KD * HT].rearrange("p (k t) -> p k t", k=KD)
        o += KD * HT
        xnT = arena[:, o:o + KD * COLS].rearrange("p (k t) -> p k t", k=KD)
        ring = arena[:, 0:RING * D].rearrange("p (r d) -> p r d", r=RING)
        proj = sb("proj", [P, CT, COLS])
        tA = sb("tA", [P, COLS])
        tB = sb("tB", [P, COLS])
        std = sb("std", [P, 2 * HT])
        rstd = sb("rstd", [P, 2 * HT])
        xt = sb("xt", [P, 2, D])
        h2b = sb("h2b", [P, 2, D])
        xfb = sb("xfb", [P, 2, D])
        junk = sb("junk", [P, 2, D])
        scores = sb("scores", [P, HP * KEYS])
        work = sb("work", [P, 2 * KEYS * 2])
        onehot = sb("onehot", [P, TOPK * TOPK])
        col = sb("col", [P, 16])
        smalls = sb("smalls", [P, 32])
        skT = sb("skT", [P, HP * KEYS])
        poolw = sb("poolw", [P, NG, P])
        grow = sb("grow", [P, 2, D])
        ident = sb("ident", [P, P])
        ones = sb("ones", [P, P])
        iota = sb("iota", [P, TOPK])
        tops = sb("tops", [P, HP, TOPK])
        topi = sb("topi", [P, HP, TOPK], U32)
        best = sb("best", [P, HEADS, TOPK])
        pos = sb("pos", [P, HEADS, TOPK], U32)
        digit = sb("digit", [P, 2, TOPK], U32)
        half_i = sb("half_i", [P, 2, HK])
        gexp = sb("gexp", [P, HEADS, TOPK])
        gsum = sb("gsum", [P, 2, HEADS])
        idx = sb("idx", [P, HK], U32)
        gates = sb("gates", [P, HK])
        dots = sb("dots", [P, HK])
        gelu = sb("gelu", [P, HK])
        weight = sb("weight", [P, HK])
        acc = sb("acc", [P, 2, D])
        psum = ctx.enter_context(nc.psum_tensor("pairs", [P, PAIRS, 2 * HT], FP32))

        g_mix, pscale = smalls[:, 0:8], smalls[:, 8:12]
        convw = smalls[:, 12:24].rearrange("p (w c) -> p w c", w=3)
        g_ab = smalls[:, 24:32]
        eps = col[:, 0:1]

        const_in = sem("const_in")
        const_dve = sem("const_dve")
        const_pool = sem("const_pool")
        w_loaded = [sem(f"w_loaded{i}") for i in range(2)]
        w_used = sem("w_used")
        xT_loaded = sem("xT_loaded")
        xt_loaded = [sem(f"xt_loaded{i}") for i in range(2)]
        squares = sem("squares")
        pe_step = sem("pe_step")
        act_emptied = sem("act_emptied")
        dve_emptied = sem("dve_emptied")
        emptied = {"act": act_emptied, "dve": dve_emptied}
        std_ready = sem("std_ready")
        xn_ready = sem("xn_ready")
        pooled = sem("pooled")
        conv_done = sem("conv_done")
        y_ready = sem("y_ready")
        xf_ready = sem("xf_ready")
        kept = [sem(f"kept{i}") for i in range(2)]
        scores_kept = sem("scores_kept")
        s_loaded = sem("s_loaded")
        s_used = sem("s_used")
        blk_loaded = sem("blk_loaded")
        blk_used = sem("blk_used")
        routed = sem("routed")
        shifted = sem("shifted")
        exped = sem("exped")
        row_in = [sem(f"row_in{i}") for i in range(RING)]
        rows_used = sem("rows_used")
        pool_go = sem("pool_go")
        sp_go = sem("sp_go")
        act_go = sem("act_go")
        gelu_done = sem("gelu_done")
        h3_ready = sem("h3_ready")
        root_done = sem("root_done")
        out_ready = sem("out_ready")
        out_kept = sem("out_kept")

        block = ctx.enter_context(nc.Block())

        @block.sync
        def _(sp):
            sp.dma_start(smalls[:], small).then_inc(const_in, 16)
            sp.dma_start(skT[:], sub_keys).then_inc(const_in, 16)
            sp.dma_start(poolw[:].rearrange("p g n -> p (g n)"), pool_w).then_inc(const_in, 16)
            sp.dma_start(grow[:].rearrange("p g n -> p (g n)"), rows_g).then_inc(const_in, 16)
            with sp.Fori(0, HALVES) as h:
                sp.wait_ge(pe_step, h * NSTEP + 1)
                sp.sem_inc(sp_go, 1)
                sp.dma_start(xnT, hT[:, :, bass.ds(h * HT, COLS)]).then_inc(xT_loaded, 16)
                for n in range(LOADS):
                    if n == 6:
                        for t in range(TT):
                            sp.wait_ge(xf_ready, h * TT + t + 1)
                            sp.sem_inc(sp_go, 1)
                            row = bass.ds(h * TT + t, 1)
                            sp.dma_start(h2_d[row, :, :].rearrange("o p n -> (o p) n"), h2b[:, t % 2, :]).then_inc(kept[t % 2], 16)
                            sp.dma_start(xf_d[row, :, :].rearrange("o p n -> (o p) n"), xfb[:, t % 2, :]).then_inc(kept[t % 2], 16)
                    sp.wait_ge(w_used, h * LOADS + n + 1)
                    sp.sem_inc(sp_go, 1)
                    src = w_in if n < 4 else w_out if n < 6 else w_query
                    c = (n if n < 4 else n - 4 if n < 6 else n - 6) * SLOTW
                    sp.dma_start(wslot[n % 2], src[:, :, c:c + SLOTW]).then_inc(w_loaded[n % 2], 16)
                for t in range(TT):
                    _, until = emptied_until(position["score", 2 * t + 1])
                    sp.wait_ge(act_emptied, (h + 1) * per_half["act"] + until)
                    sp.sem_inc(sp_go, 1)
                    sp.dma_start(s_d[bass.ds(h * TT + t, 1), :, :].rearrange("o p n -> (o p) n"), scores[:]).then_inc(scores_kept, 16)
                sp.wait_ge(scores_kept, h * (16 * TT) + 16 * TT)
                sp.wait_ge(kept[0], h * 64 + 64)
                sp.wait_ge(kept[1], h * 64 + 64)
                sp.sem_inc(sp_go, 1)

            with sp.Fori(0, TILES) as b:
                sp.wait_ge(s_used, b + 1)
                sp.wait_ge(scores_kept, 16 * TILES)
                sp.sem_inc(sp_go, 1)
                sp.dma_start(scores[:], s_d[bass.ds(b, 1), :, :].rearrange("o p n -> (o p) n")).then_inc(s_loaded, 16)
                sp.wait_ge(blk_used, b + 1)
                sp.wait_ge(kept[0], 32 * TILES // 2)
                sp.wait_ge(kept[1], 32 * TILES // 2)
                sp.sem_inc(sp_go, 1)
                sp.dma_start(xfb[:, 0, :], xf_d[bass.ds(b, 1), :, :].rearrange("o p n -> (o p) n")).then_inc(blk_loaded, 16)
                sp.dma_start(h2b[:, 0, :], h2_d[bass.ds(b, 1), :, :].rearrange("o p n -> (o p) n")).then_inc(blk_loaded, 16)

        @block.gpsimd
        def _(pool):
            pool.wait_ge(const_dve, 1)
            nc.gpsimd.affine_select(out=ident[:], in_=ident[:], compare_op=ALU.is_equal, fill=0.0, base=0,
                                    pattern=[[-1, P]], channel_multiplier=1).then_inc(const_pool, 1)
            nc.gpsimd.iota(iota[:], [[1, TOPK]], base=0, channel_multiplier=0,
                           allow_small_or_imprecise_dtypes=True).then_inc(const_pool, 1)
            with pool.Fori(0, TILES) as b:
                pool.wait_ge(routed, b + 1)
                pool.sem_inc(pool_go, 1)
                for n in range(2 * HK):
                    pool.wait_ge(rows_used, b * (2 * HK) + n + 1)
                    pool.sem_inc(pool_go, 1)
                    k = n % HK
                    nc.gpsimd.indirect_dma_start(
                        out=ring[:, n % RING, :], out_offset=None, in_=expert_u if n < HK else expert_v,
                        in_offset=bass.IndirectOffsetOnAxis(ap=idx[:, k:k + 1], axis=0)).then_inc(row_in[n % RING], 16)

        @block.tensor
        def _(pe):
            pe.sem_inc(w_used, 2)
            pe.sem_inc(pe_step, 1)
            pe.wait_ge(const_in, 64)
            pe.wait_ge(const_dve, 2)
            pe.wait_ge(const_pool, 2)
            with pe.Fori(0, HALVES) as h:
                def pair_free(n):
                    e, until = emptied_until((n - PAIRS) % NSTEP)
                    pe.wait_ge(emptied[e], (h + (n >= PAIRS)) * per_half[e] + until)

                load = [0]

                def next_slot():
                    n = load[0]
                    load[0] += 1
                    pe.wait_ge(w_loaded[n % 2], h * (16 * LOADS // 2) + 16 * (n // 2 + 1))
                    return wslot[n % 2]

                for n, (kind, i, _) in enumerate(steps):
                    pair = psum[:, n % PAIRS, :]
                    pair_free(n)
                    if kind == "sumsq":
                        pe.wait_ge(squares, h * 2 + 1)
                        for c in range(2):
                            for k in range(KD):
                                last = nc.tensor.matmul(pair[:, c * HT:c * HT + HB], ones[:], proj[:, k, c * HB:(c + 1) * HB],
                                                        start=(k == 0), stop=(k == KD - 1))
                    elif kind == "proj":
                        if i % 4 == 0:
                            w = next_slot()
                        for c in range(2):
                            for k in range(KD):
                                if i == 0 and c == 0:
                                    pe.wait_ge(xn_ready, h * KD + k + 1)
                                last = nc.tensor.matmul(pair[:, c * HT:c * HT + HB], w[:, k, (i % 4) * P:(i % 4 + 1) * P],
                                                        xnT[:, k, c * HB:(c + 1) * HB], start=(k == 0), stop=(k == KD - 1))
                        if i % 4 == 3:
                            pe.drain()
                            pe.sem_inc(w_used, 1)
                    elif kind == "pool":
                        for c in range(2):
                            pe.wait_ge(pooled, h * NG + 2 * i + c + 1)
                            last = nc.tensor.matmul(pair[:, c * HT:(c + 1) * HT], poolw[:, 2 * i + c, :], yT[:, 2 * i + c, :],
                                                    start=True, stop=True)
                    elif kind == "ynorm":
                        pe.wait_ge(squares, h * 2 + 2)
                        for c in range(2):
                            for k in range(NG):
                                last = nc.tensor.matmul(pair[:, c * HT:(c + 1) * HT], ones[:], xnT[:, c * NG + k, 0:HT],
                                                        start=(k == 0), stop=(k == NG - 1))
                    elif kind == "outp":
                        if i == 0:
                            wo = [next_slot(), next_slot()]
                            pe.wait_ge(y_ready, h * KD + KD)
                        for c in range(2):
                            for k in range(KD):
                                last = nc.tensor.matmul(pair[:, c * HT:(c + 1) * HT], yT[:, k, i * P:(i + 1) * P], wo[c][:, k, :],
                                                        start=(k == 0), stop=(k == KD - 1))
                        if i == TT - 1:
                            pe.drain()
                            pe.sem_inc(w_used, 2)
                    elif kind == "turn":
                        pe.wait_ge(xf_ready, h * TT + i + 1)
                        for k in range(KD):
                            last = nc.tensor.transpose(pair[:, k * P:(k + 1) * P], xfb[:, i % 2, k * P:(k + 1) * P], ident[:])
                    elif kind == "query":
                        if i == 0:
                            e, until = emptied_until(position["turn", TT - 1])
                            pe.wait_ge(emptied[e], (h + 1) * per_half[e] + until)
                        if i % 2 == 0:
                            w = next_slot()
                        for c in range(2):
                            m = (2 * i + c) % 4
                            for k in range(KD):
                                last = nc.tensor.matmul(pair[:, c * HT:(c + 1) * HT], w[:, k, m * P:(m + 1) * P], xnT[:, k, 0:HT],
                                                        start=(k == 0), stop=(k == KD - 1))
                        if i % 2 == 1:
                            pe.drain()
                            pe.sem_inc(w_used, 1)
                    elif kind == "score":
                        if i == 0:
                            e, until = emptied_until(position["query", CT // 2 - 1])
                            pe.wait_ge(emptied[e], (h + 1) * per_half[e] + until)
                        t, m = i // 2, i % 2
                        for c in range(HEADS):
                            hp = m * HEADS + c
                            last = nc.tensor.matmul(pair[:, c * KEYS:(c + 1) * KEYS], proj[:, hp, t * P:(t + 1) * P],
                                                    skT[:, hp * KEYS:(hp + 1) * KEYS], start=True, stop=True)
                    last.then_inc(pe_step, 1)

        @block.scalar
        def _(act):
            act.sem_inc(act_emptied, per_half["act"])
            act.wait_ge(const_in, 64)
            act.wait_ge(const_dve, 3)
            with act.Fori(0, HALVES) as h:
                def full(kind, i):
                    act.wait_ge(pe_step, h * NSTEP + position[kind, i] + 2)
                    return psum[:, position[kind, i] % PAIRS, :]

                act.wait_ge(dve_emptied, h * TT + TT)
                for t in range(2):
                    act.dma_start(xt[:, t, :], x[bass.ds(h * TT + t, 1), :, :].rearrange("o p n -> (o p) n")).then_inc(xt_loaded[t], 16)
                act.wait_ge(xT_loaded, h * 16 + 16)
                act.wait_ge(pe_step, h * NSTEP + 1)
                for k in range(KD):
                    last = nc.scalar.activation(proj[:, k, :], xnT[:, k, :], ACT.Square)
                last.then_inc(squares, 1)
                pair = full("sumsq", 0)
                nc.scalar.activation(std[:, 0:COLS].rearrange("p (c t) -> p c t", c=2),
                                     pair.rearrange("p (c t) -> p c t", c=2)[:, :, 0:HB], ACT.Sqrt,
                                     bias=eps, scale=1.0 / D).then_inc(act_emptied, 1)
                for i in range(CT):
                    pair = full("proj", i)
                    nc.scalar.activation(proj[:, i, :].rearrange("p (c t) -> p c t", c=2),
                                         pair.rearrange("p (c t) -> p c t", c=2)[:, :, 0:HB], ACT.Copy).then_inc(act_emptied, 1)
                for i in range(2):
                    pair = full("pool", i)
                    for c in range(2):
                        g = 2 * i + c
                        last = nc.scalar.activation(proj[:, g, 0:HT], pair[:, c * HT:(c + 1) * HT], ACT.Copy, scale=pscale[:, g:g + 1])
                    last.then_inc(act_emptied, 1)
                act.drain()
                for g in range(NG):
                    nc.scalar.activation(xnT[:, g, 0:HT], proj[:, g, 0:HT], ACT.Square)
                for g in range(NG):
                    act.wait_ge(conv_done, h * NG + g + 1)
                    last = nc.scalar.activation(xnT[:, NG + g, 0:HT], proj[:, 12 + g, 0:HT], ACT.Square)
                last.then_inc(squares, 1)
                pair = full("ynorm", 0)
                nc.scalar.activation(std[:], pair, ACT.Sqrt, bias=eps, scale=1.0 / (NG * P)).then_inc(act_emptied, 1)
                for t in range(TT):
                    act.wait_ge(dve_emptied, (h + 1) * TT + t + 1)
                    nc.scalar.activation(junk[:, t % 2, :], h2b[:, t % 2, :], ACT.Square, accum_out=col[:, 1 + t:2 + t])
                    act.drain()
                    nc.scalar.activation(col[:, 5 + t:6 + t], col[:, 1 + t:2 + t], ACT.Sqrt, bias=eps, scale=1.0 / D).then_inc(std_ready, 1)
                    if t < 2:
                        act.dma_start(xt[:, t, :], x[bass.ds(h * TT + t + 2, 1), :, :].rearrange("o p n -> (o p) n")).then_inc(xt_loaded[t], 16)
                for t in range(TT):
                    pair = full("turn", t)
                    nc.scalar.activation(xnT[:, :, t * P:(t + 1) * P], pair.rearrange("p (k t) -> p k t", k=KD), ACT.Copy).then_inc(act_emptied, 1)
                act.wait_ge(y_ready, h * KD + KD)
                for i in range(CT // 2):
                    pair = full("query", i)
                    nc.scalar.activation(proj[:, 2 * i:2 * i + 2, 0:HT], pair.rearrange("p (c t) -> p c t", c=2), ACT.Copy).then_inc(act_emptied, 1)
                for i in range(2 * TT):
                    pair = full("score", i)
                    if i % 2 == 0 and i > 0:
                        act.wait_ge(scores_kept, h * (16 * TT) + 16 * (i // 2))
                    nc.scalar.activation(scores[:, (i % 2) * D:(i % 2 + 1) * D], pair, ACT.Copy).then_inc(act_emptied, 1)

            with act.Fori(0, TILES) as b:
                act.wait_ge(shifted, b + 1)
                nc.scalar.activation(gexp[:].rearrange("p h k -> p (h k)"), weight[:], ACT.Exp).then_inc(exped, 1)
                act.wait_ge(rows_used, b * (2 * HK) + CREDIT + HK)
                nc.scalar.activation(gelu[:], dots[:], ACT.Gelu).then_inc(gelu_done, 1)
                act.wait_ge(h3_ready, b + 1)
                nc.scalar.activation(junk[:, 1, :], acc[:, 0, :], ACT.Square, accum_out=col[:, 9:10])
                act.drain()
                nc.scalar.activation(col[:, 10:11], col[:, 9:10], ACT.Sqrt, bias=eps, scale=1.0 / D).then_inc(root_done, 1)
                act.wait_ge(out_ready, b + 1)
                act.dma_start(out[bass.ds(b, 1), :, :].rearrange("o p n -> (o p) n"), acc[:, 1, :]).then_inc(out_kept, 16)
            act.wait_ge(out_kept, 16 * TILES)

        @block.vector
        def _(dve):
            nc.vector.memset(ident[:], 1.0).then_inc(const_dve, 1)
            nc.vector.memset(ones[:], 1.0).then_inc(const_dve, 1)
            nc.vector.memset(eps, EPS).then_inc(const_dve, 1)
            dve.sem_inc(dve_emptied, per_half["dve"])
            dve.sem_inc(rows_used, CREDIT)
            dve.wait_ge(const_in, 64)
            with dve.Fori(0, HALVES) as h:
                def act_has(kind, i):
                    _, until = emptied_until(position[kind, i])
                    dve.wait_ge(act_emptied, (h + 1) * per_half["act"] + until)

                act_has("sumsq", 0)
                nc.vector.reciprocal(rstd[:, 0:COLS], std[:, 0:COLS])
                dve.drain()
                for k in range(KD):
                    nc.vector.scalar_tensor_tensor(out=xnT[:, k, :], in0=xnT[:, k, :], scalar=g_mix[:, k:k + 1],
                                                   in1=rstd[:, 0:COLS], op0=ALU.mult, op1=ALU.mult).then_inc(xn_ready, 1)
                for g in range(NG):
                    act_has("proj", g)
                    a = proj[:, g, :]
                    src, width = a, 1
                    for r in range(g + 1):
                        dst = (tA if r % 2 == 0 else tB)[:]
                        nc.vector.tensor_tensor(dst[:, 2 * width - 1:COLS], src[:, 2 * width - 1:COLS],
                                                src[:, width - 1:COLS - width], ALU.add)
                        dve.drain()
                        src, width = dst, 2 * width
                    nc.vector.scalar_tensor_tensor(out=yT[:, g, :], in0=src[:, META:COLS], scalar=1.0 / width,
                                                   in1=a[:, META:COLS], op0=ALU.mult, op1=ALU.subtract).then_inc(pooled, 1)
                    dve.drain()
                for g in range(NG):
                    act_has("proj", 12 + g)
                    b_gate, c_gate, val = (proj[:, 4 * q + g, :] for q in (1, 2, 3))
                    nc.vector.tensor_tensor(c_gate, c_gate, val, ALU.mult)
                    dve.drain()
                    nc.vector.tensor_scalar(tA[:, META:COLS], c_gate[:, META - 2:COLS - 2], convw[:, 0, g:g + 1], None, ALU.mult)
                    dve.drain()
                    nc.vector.scalar_tensor_tensor(out=tB[:, META:COLS], in0=c_gate[:, META - 1:COLS - 1], scalar=convw[:, 1, g:g + 1],
                                                   in1=tA[:, META:COLS], op0=ALU.mult, op1=ALU.add)
                    dve.drain()
                    nc.vector.scalar_tensor_tensor(out=tA[:, META:COLS], in0=c_gate[:, META:COLS], scalar=convw[:, 2, g:g + 1],
                                                   in1=tB[:, META:COLS], op0=ALU.mult, op1=ALU.add)
                    dve.drain()
                    nc.vector.tensor_tensor(val[:, 0:HT], b_gate[:, META:COLS], tA[:, META:COLS], ALU.mult).then_inc(conv_done, 1)
                act_has("ynorm", 0)
                nc.vector.reciprocal(rstd[:], std[:])
                dve.drain()
                for k in range(KD):
                    src = proj[:, k if k < NG else 8 + k, 0:HT]
                    r = rstd[:, 0:HT] if k < NG else rstd[:, HT:2 * HT]
                    nc.vector.scalar_tensor_tensor(out=yT[:, k, :], in0=src, scalar=g_ab[:, k:k + 1], in1=r,
                                                   op0=ALU.mult, op1=ALU.mult).then_inc(y_ready, 1)
                for t in range(TT):
                    n = position["outp", t]
                    dve.wait_ge(pe_step, h * NSTEP + n + 2)
                    dve.wait_ge(xt_loaded[t % 2], h * 32 + 16 * (t // 2) + 16)
                    if t >= 2:
                        dve.wait_ge(kept[t % 2], h * 64 + 32 * (t // 2))
                    nc.vector.tensor_tensor(h2b[:, t % 2, :], psum[:, n % PAIRS, :], xt[:, t % 2, :], ALU.add).then_inc(dve_emptied, 1)
                    dve.wait_ge(std_ready, h * TT + t + 1)
                    nc.vector.reciprocal(col[:, 11 + t % 2:12 + t % 2], col[:, 5 + t:6 + t])
                    dve.drain()
                    if t >= 2:
                        dve.wait_ge(pe_step, h * NSTEP + position["turn", t - 2] + 2)
                    nc.vector.scalar_tensor_tensor(out=xfb[:, t % 2, :], in0=h2b[:, t % 2, :], scalar=col[:, 11 + t % 2:12 + t % 2],
                                                   in1=grow[:, 0, :], op0=ALU.mult, op1=ALU.mult).then_inc(xf_ready, 1)

            def rank_keys(hp):
                s = scores[:, hp * KEYS:(hp + 1) * KEYS]
                rest = work[:, 0:KEYS]
                nc.vector.max(tops[:, hp, 0:8], s)
                dve.drain()
                nc.vector.max_index(topi[:, hp, 0:8], tops[:, hp, 0:8], s)
                nc.vector.match_replace(rest, tops[:, hp, 0:8], s, LOWEST)
                dve.drain()
                nc.vector.max(tops[:, hp, 8:16], rest)
                dve.drain()
                nc.vector.max_index(topi[:, hp, 8:16], tops[:, hp, 8:16], rest)
                dve.drain()

            def rank_pairs(hd):
                cand = work[:, 0:256]
                rest = work[:, 256:512]
                nc.vector.tensor_tensor(cand.rearrange("p (a b) -> p a b", a=TOPK),
                                        tops[:, 2 * hd, :].unsqueeze(2).to_broadcast([P, TOPK, TOPK]),
                                        tops[:, 2 * hd + 1, :].unsqueeze(1).to_broadcast([P, TOPK, TOPK]), ALU.add)
                dve.drain()
                nc.vector.max(best[:, hd, 0:8], cand)
                dve.drain()
                nc.vector.max_index(pos[:, hd, 0:8], best[:, hd, 0:8], cand)
                nc.vector.match_replace(rest, best[:, hd, 0:8], cand, LOWEST)
                dve.drain()
                nc.vector.max(best[:, hd, 8:16], rest)
                dve.drain()
                nc.vector.max_index(pos[:, hd, 8:16], best[:, hd, 8:16], rest)
                dve.drain()
                nc.vector.tensor_scalar(digit[:, 0, :], pos[:, hd, :], 4, None, ALU.logical_shift_right)
                nc.vector.tensor_scalar(digit[:, 1, :], pos[:, hd, :], TOPK - 1, None, ALU.bitwise_and)
                dve.drain()
                hot = onehot[:].rearrange("p (k a) -> p k a", k=TOPK)
                for side in range(2):
                    nc.vector.tensor_tensor(hot, digit[:, side, :].unsqueeze(2).to_broadcast([P, TOPK, TOPK]),
                                            iota[:].unsqueeze(1).to_broadcast([P, TOPK, TOPK]), ALU.is_equal)
                    dve.drain()
                    nc.vector.tensor_tensor(hot, hot, topi[:, 2 * hd + side, :].unsqueeze(1).to_broadcast([P, TOPK, TOPK]), ALU.mult)
                    dve.drain()
                    nc.vector.tensor_reduce(half_i[:, side, hd * TOPK:(hd + 1) * TOPK], hot, AX.X, ALU.add)
                    dve.drain()

            def hand_over():
                nc.vector.tensor_tensor(weight[:].rearrange("p (h k) -> p h k", h=HEADS), best[:],
                                        best[:, :, 0:1].to_broadcast([P, HEADS, TOPK]), ALU.subtract).then_inc(shifted, 1)
                nc.vector.scalar_tensor_tensor(out=idx[:], in0=half_i[:, 0, :], scalar=float(KEYS), in1=half_i[:, 1, :],
                                               op0=ALU.mult, op1=ALU.add).then_inc(routed, 1)

            def normalise(b):
                dve.wait_ge(exped, b + 1)
                nc.vector.tensor_reduce(gsum[:, 0, :], gexp[:], AX.X, ALU.add)
                dve.drain()
                nc.vector.reciprocal(gsum[:, 1, :], gsum[:, 0, :])
                dve.drain()
                nc.vector.tensor_tensor(gates[:].rearrange("p (h k) -> p h k", h=HEADS), gexp[:],
                                        gsum[:, 1, :].unsqueeze(2).to_broadcast([P, HEADS, TOPK]), ALU.mult)
                dve.drain()

            def expert_block(b, rank_next):
                normalise(b)
                dve.wait_ge(blk_loaded, b * 32 + 32)
                for n in range(2 * HK):
                    k = n % HK
                    if n == HK:
                        dve.wait_ge(gelu_done, b + 1)
                        nc.vector.tensor_tensor(weight[:], gelu[:], gates[:], ALU.mult)
                        dve.drain()
                    row = ring[:, n % RING, :]
                    dve.wait_ge(row_in[n % RING], b * (16 * 2 * HK // RING) + 16 * (n // RING) + 16)
                    dve.wait_ge(rows_used, b * (2 * HK) + n + CREDIT - 1)
                    if n < HK:
                        nc.vector.tensor_tensor_reduce(out=junk[:, n % 2, :], in0=row, in1=xfb[:, 0, :], scale=1.0, scalar=0.0,
                                                       op0=ALU.mult, op1=ALU.add, accum_out=dots[:, k:k + 1]).then_inc(rows_used, 1)
                    elif k < 2:
                        nc.vector.tensor_scalar(acc[:, k, :], row, weight[:, k:k + 1], None, ALU.mult).then_inc(rows_used, 1)
                    else:
                        nc.vector.scalar_tensor_tensor(out=acc[:, k % 2, :], in0=row, scalar=weight[:, k:k + 1], in1=acc[:, k % 2, :],
                                                       op0=ALU.mult, op1=ALU.add).then_inc(rows_used, 1)
                    if rank_next:
                        if n == 0:
                            dve.wait_ge(s_loaded, b * 16 + 32)
                        if n < HK and k % 8 == 7:
                            rank_keys(k // 8)
                            if k == HK - 1:
                                dve.sem_inc(s_used, 1)
                        if n >= HK and k % 16 == 15:
                            rank_pairs(k // 16)
                dve.drain()
                nc.vector.tensor_tensor(acc[:, 0, :], acc[:, 0, :], acc[:, 1, :], ALU.add)
                if rank_next:
                    hand_over()
                dve.drain()
                nc.vector.tensor_tensor(acc[:, 0, :], acc[:, 0, :], h2b[:, 0, :], ALU.add).then_inc(h3_ready, 1)
                dve.drain()
                dve.sem_inc(blk_used, 1)
                dve.wait_ge(root_done, b + 1)
                nc.vector.reciprocal(col[:, 13:14], col[:, 10:11])
                dve.drain()
                nc.vector.scalar_tensor_tensor(out=acc[:, 1, :], in0=acc[:, 0, :], scalar=col[:, 13:14], in1=grow[:, 1, :],
                                               op0=ALU.mult, op1=ALU.mult).then_inc(out_ready, 1)
                dve.wait_ge(out_kept, b * 16 + 16)

            dve.wait_ge(const_pool, 2)
            dve.sem_inc(blk_used, 1)
            dve.sem_inc(s_used, 1)
            dve.wait_ge(s_loaded, 16)
            for hp in range(HP):
                rank_keys(hp)
            dve.sem_inc(s_used, 1)
            for hd in range(HEADS):
                rank_pairs(hd)
            hand_over()
            dve.drain()
            with dve.Fori(0, TILES - 1) as b:
                expert_block(b, True)
            expert_block(TILES - 1, False)


def kernel(x, meta_tokens, norm_mix_g, w_in, pool_w, pool_scale, conv_w, norm_a_g, norm_b_g, w_out, norm_ffn_g,
           w_query, sub_keys, expert_u, expert_v, norm_final_g):
    import numpy as np
    import concourse.bacc as bacc
    from concourse.bass_utils import run_bass_kernel_spmd

    a = lambda v: np.asarray(v)
    tiles_first = lambda w: np.ascontiguousarray(w.reshape(KD, P, -1).transpose(1, 0, 2))
    per_partition = lambda v: v.reshape(-1, P).T
    x2 = a(x)[0]
    h = np.concatenate([a(meta_tokens), x2], axis=0)
    small = np.concatenate([per_partition(a(norm_mix_g)[0]), per_partition(a(pool_scale)[0]),
                            per_partition(a(conv_w)[0].reshape(-1)), per_partition(a(norm_a_g)[0]),
                            per_partition(a(norm_b_g)[0])], axis=1)
    rows_g = np.concatenate([a(norm_ffn_g)[0], a(norm_final_g)])[None, :].repeat(P, axis=0)
    arrays = {
        "hT": tiles_first(h.T),
        "x": x2.reshape(TILES, P, D),
        "w_in": tiles_first(a(w_in)[0]),
        "w_out": tiles_first(a(w_out)[0]),
        "w_query": tiles_first(a(w_query)[0]),
        "sub_keys": a(sub_keys)[0].transpose(3, 0, 1, 2).reshape(P, HP * KEYS),
        "pool_w": a(pool_w)[0].transpose(1, 0, 2).reshape(P, NG * P),
        "small": small,
        "rows_g": rows_g,
        "expert_u": a(expert_u)[0],
        "expert_v": a(expert_v)[0],
    }
    arrays = {f"in_{n}": np.ascontiguousarray(v) for n, v in arrays.items()}
    nc = bacc.Bacc("TRN2", target_bir_lowering=False, num_devices=1)
    args = [nc.dram_tensor(n, v.shape, mybir.dt.from_np(v.dtype), kind="ExternalInput").ap() for n, v in arrays.items()]
    result = nc.dram_tensor("out", (TILES, P, D), FP32, kind="ExternalOutput").ap()
    program(nc, *args, result)
    r = run_bass_kernel_spmd(nc, [arrays], core_ids=[0])
    return r.results[0]["out"].reshape(1, SEQ, D)
```

```python
import concourse.bass as bass
from concourse import mybir
from concourse.alu_op_type import AluOpType as ALU
from contextlib import ExitStack
import numpy as np

FP32 = mybir.dt.float32
U32 = mybir.dt.uint32
BF16 = mybir.dt.bfloat16
ACT = mybir.ActivationFunctionType
AX = mybir.AxisListType

P = 128
D = 1024
KD = D // P
SEQ, META = 1024, 16
HALVES = 2
HT = SEQ // HALVES
TT = HT // P
TILES = SEQ // P
COLS = HT + META
HB = COLS // 2
CT = 16
NG = 4
HEADS, KEYS, TOPK = 8, 128, 16
HP = 2 * HEADS
HK = HEADS * TOPK
SLOTW = 512
EPS = 1e-6
LOWEST = -3.0e38
DENSE_TILES = TT
BLOCKS = TILES - DENSE_TILES
RING = 8
GJ = 8
GROUPS = KEYS // GJ
PER_BLOCK = GROUPS // BLOCKS
ITEMS = 2 * GJ * PER_BLOCK
EVERY = 2 * HK // ITEMS
SUMS = 2 * DENSE_TILES
assert SUMS == GJ
USLOTS = 4
HOTS = 8
CHUNK = 32


def program(nc, hT, x, w_in, w_out, w_query, sub_keys, pool_w, small, rows_g, expert_u, expert_v, uT, out):
    h2_d = nc.dram_tensor("h2_scratch", (TILES, P, D), FP32, kind="Internal").ap()
    xf_d = nc.dram_tensor("xf_scratch", (TILES, P, D), FP32, kind="Internal").ap()
    s_d = nc.dram_tensor("score_scratch", (TILES, P, HP * KEYS), FP32, kind="Internal").ap()
    xfT_d = nc.dram_tensor("xfT_scratch", (HALVES, P, KD, HT), FP32, kind="Internal").ap()
    g_d = nc.dram_tensor("gate_tables", (GROUPS, P, HT * GJ), FP32, kind="Internal").ap()
    v_rows = expert_v.rearrange("(i j) d -> i (j d)", j=KEYS)

    steps = ([("sumsq", 0, "act")] + [("proj", c, "act") for c in range(CT)]
             + [("pool", i, "act") for i in range(2)] + [("ynorm", 0, "act")]
             + [("outp", t, "dve") for t in range(TT)] + [("turn", t, "act") for t in range(TT)]
             + [("query", c, "act") for c in range(CT // 2)] + [("score", i, "act") for i in range(2 * TT)])
    NSTEP = len(steps)
    PAIRS = 4
    assert NSTEP % PAIRS == 0
    position = {(kind, i): n for n, (kind, i, _) in enumerate(steps)}
    per_half = {e: sum(s[2] == e for s in steps) for e in ("act", "dve")}

    def emptied_until(n):
        e = steps[n][2]
        return e, sum(s[2] == e for s in steps[:n + 1])

    LOADS = 10

    ctx = ExitStack()
    with ctx:
        def sb(name, shape, dt=FP32):
            return ctx.enter_context(nc.sbuf_tensor(name, shape, dt))

        def sem(name):
            return ctx.enter_context(nc.semaphore(name))

        arena = sb("arena", [P, 43008])
        views = {}

        def place(names):
            o = 0
            for name, shape in names:
                n = int(np.prod(shape))
                v = arena[:, o:o + n]
                if len(shape) > 1:
                    v = v.rearrange("p (a b) -> p a b", a=shape[0])
                views[name] = v
                o += n
            assert o <= 43008, o

        place([("wslot0", (KD, SLOTW)), ("wslot1", (KD, SLOTW)), ("yT", (KD, HT)), ("xnT", (KD, COLS)), ("proj", (CT, COLS)),
               ("tA", (COLS,)), ("tB", (COLS,)), ("std", (2 * HT,)), ("rstd", (2 * HT,)), ("xt", (2, D)), ("h2b", (2, D)),
               ("xfb", (2, D)), ("squared", (D,)), ("scores", (HP * KEYS,)), ("skT", (HP * KEYS,)), ("poolw", (NG, P)),
               ("g_ffn", (D,))])
        place([("uslot", (USLOTS, D)), ("vrows", (GJ, D)), ("gtab", (HT * GJ,)), ("gated", (GJ, HT)),
               ("sums", (DENSE_TILES, D)), ("xfT", (KD, HT)), ("acts", (2, HT)), ("ring", (RING, D)), ("xf", (D,)),
               ("h2", (D,)), ("acc", (2, D)), ("junk32", (D,))])
        wslot = [views["wslot0"], views["wslot1"]]
        yT, xnT, proj, tA, tB, std, rstd, xt, h2b, xfb, squared, scores, skT, poolw, g_ffn = (views[n] for n in (
            "yT", "xnT", "proj", "tA", "tB", "std", "rstd", "xt", "h2b", "xfb", "squared", "scores", "skT", "poolw", "g_ffn"))
        uslot, vrows, gtab, gated, sums, xfT, acts, ring, xf, h2, acc = (views[n] for n in (
            "uslot", "vrows", "gtab", "gated", "sums", "xfT", "acts", "ring", "xf", "h2", "acc"))
        junk = views["junk32"].bitcast(BF16).rearrange("p (r d) -> p r d", r=2)
        hots = gated.rearrange("p a b -> p (a b)").rearrange("p (c s t j) -> p c s t j", c=2, s=2, j=KEYS)
        tables = vrows.rearrange("p a b -> p (a b)").rearrange("p (c g t j) -> p c g t j", c=2, g=GROUPS, t=CHUNK)
        ranking = sb("ranking", [P, HP * KEYS])
        work = sb("work", [P, 4 * KEYS])
        col = sb("col", [P, 16])
        smalls = sb("smalls", [P, 32])
        g_final = sb("g_final", [P, D])
        ident = sb("ident", [P, P])
        ones = sb("ones", [P, P])
        iota = sb("iota", [P, KEYS])
        tops = sb("tops", [P, HP, TOPK])
        topi = sb("topi", [P, HP, TOPK], U32)
        best = sb("best", [P, HEADS, TOPK])
        pos = sb("pos", [P, HEADS, TOPK], U32)
        digit = sb("digit", [P, 2, 2, TOPK], U32)
        half_i = sb("half_i", [P, 2, HK])
        route = sb("route", [P, 3, DENSE_TILES, HK])
        routeT = sb("routeT", [P, 3, DENSE_TILES, P])
        keysT = routeT[:].rearrange("p m t k -> p m (t k)")
        gexp = sb("gexp", [P, HEADS, TOPK])
        gsum = sb("gsum", [P, 2, DENSE_TILES * HEADS])
        idx = sb("idx", [P, HK], U32)
        gates = sb("gates", [P, HK])
        dots = sb("dots", [P, HK])
        gelu = sb("gelu", [P, HK])
        weight = sb("weight", [P, HK])
        psum = ctx.enter_context(nc.psum_tensor("pairs", [P, PAIRS, 2 * HT], FP32))
        bank = [psum[:, n // 2, (n % 2) * HT:(n % 2 + 1) * HT] for n in range(8)]
        s_bank, o_bank, g_bank = bank[0:2], bank[2:6], bank[0:4]

        g_mix, pscale = smalls[:, 0:8], smalls[:, 8:12]
        convw = smalls[:, 12:24].rearrange("p (w c) -> p w c", w=3)
        g_ab = smalls[:, 24:32]
        eps = col[:, 0:1]

        const_in = sem("const_in")
        const_dve = sem("const_dve")
        const_pool = sem("const_pool")
        w_loaded = [sem(f"w_loaded{i}") for i in range(2)]
        w_used = sem("w_used")
        xT_loaded = sem("xT_loaded")
        xt_loaded = [sem(f"xt_loaded{i}") for i in range(2)]
        squares = sem("squares")
        pe_step = sem("pe_step")
        act_emptied = sem("act_emptied")
        dve_emptied = sem("dve_emptied")
        emptied = {"act": act_emptied, "dve": dve_emptied}
        std_ready = sem("std_ready")
        xn_ready = sem("xn_ready")
        pooled = sem("pooled")
        conv_done = sem("conv_done")
        y_ready = sem("y_ready")
        xf_ready = sem("xf_ready")
        kept = [sem(f"kept{i}") for i in range(2)]
        xfT_kept = sem("xfT_kept")
        scores_kept = sem("scores_kept")
        s_loaded = sem("s_loaded")
        s_used = sem("s_used")
        xf_in = sem("xf_in")
        h2_in = sem("h2_in")
        routed = sem("routed")
        shifted = sem("shifted")
        exped = sem("exped")
        row_in = [sem(f"row_in{i}") for i in range(RING)]
        rows_used = sem("rows_used")
        pool_go = sem("pool_go")
        sp_go = sem("sp_go")
        act_go = sem("act_go")
        pe_go = sem("pe_go")
        dve_go = sem("dve_go")
        gelu_done = sem("gelu_done")
        h3_ready = sem("h3_ready")
        root_done = sem("root_done")
        out_ready = sem("out_ready")
        out_kept = sem("out_kept")
        mixers_done = sem("mixers_done")
        d_shifted = sem("d_shifted")
        d_exped = sem("d_exped")
        d_gates = sem("d_gates")
        turned = sem("turned")
        turned_out = sem("turned_out")
        hot_ready = sem("hot_ready")
        hot_gated = sem("hot_gated")
        table_full = sem("table_full")
        table_out = sem("table_out")
        table_kept = [sem(f"table_kept{i}") for i in range(2)]
        xfT_in = sem("xfT_in")
        u_in = [sem(f"u_in{i}") for i in range(USLOTS)]
        v_in = [sem(f"v_in{i}") for i in range(2)]
        g_in = sem("g_in")
        s_full = sem("s_full")
        act_ready = sem("act_ready")
        w_ready = sem("w_ready")
        o_full = sem("o_full")
        o_added = sem("o_added")
        d_h2_in = sem("d_h2_in")

        block = ctx.enter_context(nc.Block())

        @block.sync
        def _(sp):
            sp.dma_start(smalls[:], small).then_inc(const_in, 16)
            sp.dma_start(skT, sub_keys).then_inc(const_in, 16)
            sp.dma_start(poolw.rearrange("p g n -> p (g n)"), pool_w).then_inc(const_in, 16)
            sp.dma_start(g_ffn, rows_g[:, 0:D]).then_inc(const_in, 16)
            sp.dma_start(g_final[:], rows_g[:, D:2 * D]).then_inc(const_in, 16)
            with sp.Fori(0, HALVES) as h:
                sp.wait_ge(pe_step, h * NSTEP + 1)
                sp.sem_inc(sp_go, 1)
                sp.dma_start(xnT, hT[:, :, bass.ds(h * HT, COLS)]).then_inc(xT_loaded, 16)
                for n in range(LOADS):
                    if n == 6:
                        for t in range(TT):
                            sp.wait_ge(xf_ready, h * TT + t + 1)
                            sp.sem_inc(sp_go, 1)
                            row = bass.ds(h * TT + t, 1)
                            sp.dma_start(h2_d[row, :, :].rearrange("o p n -> (o p) n"), h2b[:, t % 2, :]).then_inc(kept[t % 2], 16)
                            sp.dma_start(xf_d[row, :, :].rearrange("o p n -> (o p) n"), xfb[:, t % 2, :]).then_inc(kept[t % 2], 16)
                        _, until = emptied_until(position["turn", TT - 1])
                        sp.wait_ge(act_emptied, (h + 1) * per_half["act"] + until)
                        sp.sem_inc(sp_go, 1)
                        sp.dma_start(xfT_d[bass.ds(h, 1), :, :, :].rearrange("o p k t -> (o p) k t"), xnT[:, :, 0:HT]).then_inc(xfT_kept, 16)
                    sp.wait_ge(w_used, h * LOADS + n + 1)
                    sp.sem_inc(sp_go, 1)
                    src = w_in if n < 4 else w_out if n < 6 else w_query
                    c = (n if n < 4 else n - 4 if n < 6 else n - 6) * SLOTW
                    sp.dma_start(wslot[n % 2], src[:, :, c:c + SLOTW]).then_inc(w_loaded[n % 2], 16)
                for t in range(TT):
                    _, until = emptied_until(position["score", 2 * t + 1])
                    sp.wait_ge(act_emptied, (h + 1) * per_half["act"] + until)
                    sp.sem_inc(sp_go, 1)
                    sp.dma_start(s_d[bass.ds(h * TT + t, 1), :, :].rearrange("o p n -> (o p) n"), scores[:]).then_inc(scores_kept, 16)
                sp.wait_ge(scores_kept, h * (16 * TT) + 16 * TT)
                sp.wait_ge(kept[0], h * 64 + 64)
                sp.wait_ge(kept[1], h * 64 + 64)
                sp.wait_ge(xfT_kept, h * 16 + 16)
                sp.sem_inc(sp_go, 1)
            sp.sem_inc(mixers_done, 1)

            sp.dma_start(xfT, xfT_d[0, :, :, :]).then_inc(xfT_in, 16)
            with sp.Fori(0, HT // (2 * CHUNK)) as it:
                for c in range(2):
                    sp.wait_ge(table_out, it * (CHUNK // 2) + (c + 1) * (CHUNK // 4) + 4)
                    sp.sem_inc(sp_go, 1)
                    sp.dma_start(g_d[:, :, bass.ds((it * 2 + c) * (CHUNK * GJ), CHUNK * GJ)].rearrange("g p n -> p g n"),
                                 tables[:, c].rearrange("p g t j -> p g (t j)")).then_inc(table_kept[c], 16)
            sp.wait_ge(table_kept[0], 16 * HT // (2 * CHUNK))
            sp.wait_ge(table_kept[1], 16 * HT // (2 * CHUNK))
            with sp.Fori(0, GROUPS) as g:
                def load_u(j):
                    sp.wait_ge(s_full, g * GJ + j + 1)
                    sp.sem_inc(sp_go, 1)
                    sp.dma_start(uslot[:, j % USLOTS, :], uT[bass.ds(g * GJ + j, 1), :, :].rearrange("o p n -> (o p) n")).then_inc(u_in[j % USLOTS], 16)

                def load_v(half):
                    sp.wait_ge(o_full, g * SUMS + 1)
                    sp.sem_inc(sp_go, 1)
                    n = GJ // 2
                    sp.dma_start(vrows[:, half * n:(half + 1) * n, :].rearrange("p j d -> p (j d)"),
                                 v_rows[:, bass.ds(g * (GJ * D) + half * (n * D), n * D)]).then_inc(v_in[half], 16)

                sp.wait_ge(w_ready, g * GJ + 2)
                sp.sem_inc(sp_go, 1)
                sp.dma_start(gtab, g_d[bass.ds(g, 1), :, :].rearrange("o p n -> (o p) n")).then_inc(g_in, 16)
                for j in range(4):
                    load_u(j)
                load_v(0)
                load_u(4)
                load_u(5)
                load_v(1)
                load_u(6)
                load_u(7)
            sp.wait_ge(rows_used, BLOCKS * 2 * HK + RING)
            sp.dma_start(ring[:, 0:DENSE_TILES, :], h2_d[0:DENSE_TILES, :, :].rearrange("t p d -> p t d")).then_inc(d_h2_in, 16)

        @block.gpsimd
        def _(pool):
            pool.wait_ge(const_dve, 1)
            nc.gpsimd.affine_select(out=ident[:], in_=ident[:], compare_op=ALU.is_equal, fill=0.0, base=0,
                                    pattern=[[-1, P]], channel_multiplier=1).then_inc(const_pool, 1)
            nc.gpsimd.iota(iota[:], [[1, KEYS]], base=0, channel_multiplier=0,
                           allow_small_or_imprecise_dtypes=True).then_inc(const_pool, 1)
            with pool.Fori(0, DENSE_TILES + 1) as t:
                pool.wait_ge(s_used, t + 1)
                pool.wait_ge(scores_kept, t * 16 + 16)
                pool.sem_inc(pool_go, 1)
                pool.dma_start(ranking[:], s_d[bass.ds(t, 1), :, :].rearrange("o p n -> (o p) n")).then_inc(s_loaded, 16)
            pool.wait_ge(turned_out, DENSE_TILES)
            with pool.Fori(0, HT // (4 * HOTS)) as it:
                for c in range(4):
                    pool.wait_ge(hot_ready, it * 4 + c + 1)
                    pool.sem_inc(pool_go, 1)
                    nc.gpsimd.tensor_tensor(hots[:, c % 2, 1], hots[:, c % 2, 1],
                                            keysT[:, 2, bass.ds((it * 4 + c) * HOTS, HOTS)].unsqueeze(2).to_broadcast([P, HOTS, KEYS]),
                                            ALU.mult).then_inc(hot_gated, 1)
            with pool.Fori(0, BLOCKS) as b:
                pool.wait_ge(routed, b + 1)
                pool.sem_inc(pool_go, 1)
                tile = lambda d: d[bass.ds(b + DENSE_TILES, 1), :, :].rearrange("o p n -> (o p) n")
                pool.wait_ge(s_used, b + DENSE_TILES + 2)
                pool.sem_inc(pool_go, 1)
                pool.dma_start(ranking[:], s_d[bass.ds((b + 1) % BLOCKS + DENSE_TILES, 1), :, :].rearrange("o p n -> (o p) n")).then_inc(s_loaded, 16)
                pool.dma_start(xf, tile(xf_d)).then_inc(xf_in, 16)
                for n in range(2 * HK):
                    if n == HK:
                        pool.wait_ge(h3_ready, b + 1)
                        pool.sem_inc(pool_go, 1)
                        pool.dma_start(h2, tile(h2_d)).then_inc(h2_in, 16)
                    pool.wait_ge(rows_used, b * (2 * HK) + n + 1)
                    pool.sem_inc(pool_go, 1)
                    k = n % HK
                    nc.gpsimd.indirect_dma_start(
                        out=ring[:, n % RING, :], out_offset=None, in_=expert_u if n < HK else expert_v,
                        in_offset=bass.IndirectOffsetOnAxis(ap=idx[:, k:k + 1], axis=0)).then_inc(row_in[n % RING], 16)

        @block.tensor
        def _(pe):
            pe.sem_inc(w_used, 2)
            pe.sem_inc(pe_step, 1)
            pe.sem_inc(table_full, 4)
            pe.wait_ge(const_in, 80)
            pe.wait_ge(const_dve, 2)
            pe.wait_ge(const_pool, 2)
            with pe.Fori(0, HALVES) as h:
                def pair_free(n):
                    e, until = emptied_until((n - PAIRS) % NSTEP)
                    pe.wait_ge(emptied[e], (h + (n >= PAIRS)) * per_half[e] + until)

                load = [0]

                def next_slot():
                    n = load[0]
                    load[0] += 1
                    pe.wait_ge(w_loaded[n % 2], h * (16 * LOADS // 2) + 16 * (n // 2 + 1))
                    return wslot[n % 2]

                for n, (kind, i, _) in enumerate(steps):
                    pair = psum[:, n % PAIRS, :]
                    pair_free(n)
                    if kind == "sumsq":
                        pe.wait_ge(squares, h * 2 + 1)
                        for c in range(2):
                            for k in range(KD):
                                last = nc.tensor.matmul(pair[:, c * HT:c * HT + HB], ones[:], proj[:, k, c * HB:(c + 1) * HB],
                                                        start=(k == 0), stop=(k == KD - 1))
                    elif kind == "proj":
                        if i % 4 == 0:
                            w = next_slot()
                        for c in range(2):
                            for k in range(KD):
                                if i == 0 and c == 0:
                                    pe.wait_ge(xn_ready, h * KD + k + 1)
                                last = nc.tensor.matmul(pair[:, c * HT:c * HT + HB], w[:, k, (i % 4) * P:(i % 4 + 1) * P],
                                                        xnT[:, k, c * HB:(c + 1) * HB], start=(k == 0), stop=(k == KD - 1))
                        if i % 4 == 3:
                            pe.drain()
                            pe.sem_inc(w_used, 1)
                    elif kind == "pool":
                        for c in range(2):
                            pe.wait_ge(pooled, h * NG + 2 * i + c + 1)
                            last = nc.tensor.matmul(pair[:, c * HT:(c + 1) * HT], poolw[:, 2 * i + c, :], yT[:, 2 * i + c, :],
                                                    start=True, stop=True)
                    elif kind == "ynorm":
                        pe.wait_ge(squares, h * 2 + 2)
                        for c in range(2):
                            for k in range(NG):
                                last = nc.tensor.matmul(pair[:, c * HT:(c + 1) * HT], ones[:], xnT[:, c * NG + k, 0:HT],
                                                        start=(k == 0), stop=(k == NG - 1))
                    elif kind == "outp":
                        if i == 0:
                            wo = [next_slot(), next_slot()]
                            pe.wait_ge(y_ready, h * KD + KD)
                        for c in range(2):
                            for k in range(KD):
                                last = nc.tensor.matmul(pair[:, c * HT:(c + 1) * HT], yT[:, k, i * P:(i + 1) * P], wo[c][:, k, :],
                                                        start=(k == 0), stop=(k == KD - 1))
                        if i == TT - 1:
                            pe.drain()
                            pe.sem_inc(w_used, 2)
                    elif kind == "turn":
                        pe.wait_ge(xf_ready, h * TT + i + 1)
                        for k in range(KD):
                            last = nc.tensor.transpose(pair[:, k * P:(k + 1) * P], xfb[:, i % 2, k * P:(k + 1) * P], ident[:])
                    elif kind == "query":
                        if i == 0:
                            e, until = emptied_until(position["turn", TT - 1])
                            pe.wait_ge(emptied[e], (h + 1) * per_half[e] + until)
                        if i % 2 == 0:
                            w = next_slot()
                        for c in range(2):
                            m = (2 * i + c) % 4
                            for k in range(KD):
                                last = nc.tensor.matmul(pair[:, c * HT:(c + 1) * HT], w[:, k, m * P:(m + 1) * P], xnT[:, k, 0:HT],
                                                        start=(k == 0), stop=(k == KD - 1))
                        if i % 2 == 1:
                            pe.drain()
                            pe.sem_inc(w_used, 1)
                    elif kind == "score":
                        if i == 0:
                            e, until = emptied_until(position["query", CT // 2 - 1])
                            pe.wait_ge(emptied[e], (h + 1) * per_half[e] + until)
                        t, m = i // 2, i % 2
                        for c in range(HEADS):
                            hp = m * HEADS + c
                            last = nc.tensor.matmul(pair[:, c * KEYS:(c + 1) * KEYS], proj[:, hp, t * P:(t + 1) * P],
                                                    skT[:, hp * KEYS:(hp + 1) * KEYS], start=True, stop=True)
                    last.then_inc(pe_step, 1)

            pe.wait_ge(d_gates, 1)
            e, until = emptied_until(NSTEP - 1)
            pe.wait_ge(emptied[e], HALVES * per_half[e] + until)
            for t in range(DENSE_TILES):
                for m in range(3):
                    last = nc.tensor.transpose(bank[4 + t][:, m * P:(m + 1) * P], route[:, m, t, :], ident[:])
                last.then_inc(turned, 1)
            with pe.Fori(0, HT // (2 * HOTS)) as it:
                for c in range(2):
                    pe.wait_ge(hot_gated, it * 2 + c + 1)
                    for m in range(2):
                        pe.wait_ge(table_out, it * 4 + 2 * c + m + 1)
                        pe.sem_inc(pe_go, 1)
                        for q in range(4):
                            last = nc.tensor.matmul(g_bank[2 * c + m][:, q * KEYS:(q + 1) * KEYS], hots[:, c, 0, 4 * m + q, :],
                                                    hots[:, c, 1, 4 * m + q, :], start=True, stop=True)
                        last.then_inc(table_full, 1)

            pe.sem_inc(s_full, USLOTS)
            pe.sem_inc(o_full, 1)
            pe.wait_ge(xfT_in, 16)
            pe.wait_ge(table_out, HT // 4 + 4)
            with pe.Fori(0, GROUPS) as g:
                for j in range(GJ):
                    pe.wait_ge(u_in[j % USLOTS], g * (16 * GJ // USLOTS) + 16 * (j // USLOTS) + 16)
                    pe.wait_ge(act_ready, g * GJ + j + 1)
                    pe.sem_inc(pe_go, 1)
                    for k in range(KD):
                        last = nc.tensor.matmul(s_bank[j % 2], uslot[:, j % USLOTS, k * P:(k + 1) * P], xfT[:, k, :],
                                                start=(k == 0), stop=(k == KD - 1))
                    last.then_inc(s_full, 1)
                for n in range(SUMS):
                    t, half = n // 2, n % 2
                    pe.wait_ge(o_added, g * SUMS + n + 1)
                    pe.sem_inc(pe_go, 1)
                    for j in range(GJ):
                        if n == 0:
                            if j % (GJ // 2) == 0:
                                pe.wait_ge(v_in[j // (GJ // 2)], g * 16 + 16)
                            pe.wait_ge(w_ready, g * GJ + j + 3)
                            pe.sem_inc(pe_go, 1)
                        last = nc.tensor.matmul(o_bank[n % 4], gated[:, j, t * P:(t + 1) * P], vrows[:, j, half * HT:(half + 1) * HT],
                                                start=(j == 0), stop=(j == GJ - 1))
                    last.then_inc(o_full, 1)

        @block.scalar
        def _(act):
            act.sem_inc(act_emptied, per_half["act"])
            act.wait_ge(const_in, 80)
            act.wait_ge(const_dve, 3)
            with act.Fori(0, HALVES) as h:
                def full(kind, i):
                    act.wait_ge(pe_step, h * NSTEP + position[kind, i] + 2)
                    return psum[:, position[kind, i] % PAIRS, :]

                act.wait_ge(dve_emptied, h * TT + TT)
                for t in range(2):
                    act.dma_start(xt[:, t, :], x[bass.ds(h * TT + t, 1), :, :].rearrange("o p n -> (o p) n")).then_inc(xt_loaded[t], 16)
                act.wait_ge(xT_loaded, h * 16 + 16)
                act.wait_ge(pe_step, h * NSTEP + 1)
                for k in range(KD):
                    last = nc.scalar.activation(proj[:, k, :], xnT[:, k, :], ACT.Square)
                last.then_inc(squares, 1)
                pair = full("sumsq", 0)
                nc.scalar.activation(std[:, 0:COLS].rearrange("p (c t) -> p c t", c=2),
                                     pair.rearrange("p (c t) -> p c t", c=2)[:, :, 0:HB], ACT.Sqrt,
                                     bias=eps, scale=1.0 / D).then_inc(act_emptied, 1)
                for i in range(CT):
                    pair = full("proj", i)
                    nc.scalar.activation(proj[:, i, :].rearrange("p (c t) -> p c t", c=2),
                                         pair.rearrange("p (c t) -> p c t", c=2)[:, :, 0:HB], ACT.Copy).then_inc(act_emptied, 1)
                for i in range(2):
                    pair = full("pool", i)
                    for c in range(2):
                        g = 2 * i + c
                        last = nc.scalar.activation(proj[:, g, 0:HT], pair[:, c * HT:(c + 1) * HT], ACT.Copy, scale=pscale[:, g:g + 1])
                    last.then_inc(act_emptied, 1)
                act.drain()
                for g in range(NG):
                    nc.scalar.activation(xnT[:, g, 0:HT], proj[:, g, 0:HT], ACT.Square)
                for g in range(NG):
                    act.wait_ge(conv_done, h * NG + g + 1)
                    last = nc.scalar.activation(xnT[:, NG + g, 0:HT], proj[:, 12 + g, 0:HT], ACT.Square)
                last.then_inc(squares, 1)
                pair = full("ynorm", 0)
                nc.scalar.activation(std, pair, ACT.Sqrt, bias=eps, scale=1.0 / (NG * P)).then_inc(act_emptied, 1)
                for t in range(TT):
                    act.wait_ge(dve_emptied, (h + 1) * TT + t + 1)
                    nc.scalar.activation(squared, h2b[:, t % 2, :], ACT.Square, accum_out=col[:, 1 + t:2 + t])
                    act.drain()
                    nc.scalar.activation(col[:, 5 + t:6 + t], col[:, 1 + t:2 + t], ACT.Sqrt, bias=eps, scale=1.0 / D).then_inc(std_ready, 1)
                    if t < 2:
                        act.dma_start(xt[:, t, :], x[bass.ds(h * TT + t + 2, 1), :, :].rearrange("o p n -> (o p) n")).then_inc(xt_loaded[t], 16)
                for t in range(TT):
                    pair = full("turn", t)
                    nc.scalar.activation(xnT[:, :, t * P:(t + 1) * P], pair.rearrange("p (k t) -> p k t", k=KD), ACT.Copy).then_inc(act_emptied, 1)
                act.wait_ge(y_ready, h * KD + KD)
                for i in range(CT // 2):
                    pair = full("query", i)
                    nc.scalar.activation(proj[:, 2 * i:2 * i + 2, 0:HT], pair.rearrange("p (c t) -> p c t", c=2), ACT.Copy).then_inc(act_emptied, 1)
                for i in range(2 * TT):
                    pair = full("score", i)
                    if i % 2 == 0 and i > 0:
                        act.wait_ge(scores_kept, h * (16 * TT) + 16 * (i // 2))
                    nc.scalar.activation(scores[:, (i % 2) * D:(i % 2 + 1) * D], pair, ACT.Copy).then_inc(act_emptied, 1)

            act.sem_inc(table_out, 4)
            act.sem_inc(act_ready, 2)
            act.wait_ge(d_shifted, 1)
            nc.scalar.activation(route[:, 2, :, :], route[:, 2, :, :], ACT.Exp).then_inc(d_exped, 1)
            for t in range(DENSE_TILES):
                act.wait_ge(turned, t + 1)
                nc.scalar.activation(routeT[:, :, t, :], bank[4 + t][:, 0:3 * P].rearrange("p (m k) -> p m k", m=3), ACT.Copy).then_inc(turned_out, 1)
            act.wait_ge(mixers_done, 1)

            def tables_out(it, first):
                for n in range(CHUNK // 2):
                    c, m = n // (CHUNK // 4), n % (CHUNK // 4)
                    if m == 0 and not first:
                        act.wait_ge(table_kept[c], it * 16)
                        act.sem_inc(act_go, 1)
                    act.wait_ge(table_full, it * (CHUNK // 2) + n + 5)
                    nc.scalar.activation(tables[:, c, :, 4 * m:4 * m + 4, :].rearrange("p g t j -> p t g j"),
                                         g_bank[n % 4].rearrange("p (t g j) -> p t g j", t=4, g=GROUPS), ACT.Copy).then_inc(table_out, 1)

            tables_out(0, True)
            with act.Fori(1, HT // (2 * CHUNK)) as it:
                tables_out(it, False)

            def gelu_tiles(b, first, count):
                for n in range(first, first + count):
                    act.wait_ge(s_full, b * (GJ * PER_BLOCK) + n + USLOTS + 1)
                    act.wait_ge(w_ready, b * (GJ * PER_BLOCK) + n + 1)
                    act.sem_inc(act_go, 1)
                    nc.scalar.activation(acts[:, n % 2, :], s_bank[n % 2], ACT.Gelu).then_inc(act_ready, 1)

            with act.Fori(0, BLOCKS) as b:
                act.wait_ge(shifted, b + 1)
                nc.scalar.activation(gexp[:].rearrange("p h k -> p (h k)"), weight[:], ACT.Exp).then_inc(exped, 1)
                gelu_tiles(b, 0, GJ * PER_BLOCK // 2)
                act.wait_ge(rows_used, b * (2 * HK) + RING + HK)
                nc.scalar.activation(gelu[:], dots[:], ACT.Gelu).then_inc(gelu_done, 1)
                gelu_tiles(b, GJ * PER_BLOCK // 2, GJ * PER_BLOCK // 2)
                act.wait_ge(h3_ready, b + 2)
                nc.scalar.activation(acc[:, 1, :], acc[:, 0, :], ACT.Square, accum_out=col[:, 9:10])
                act.drain()
                nc.scalar.activation(col[:, 10:11], col[:, 9:10], ACT.Sqrt, bias=eps, scale=1.0 / D).then_inc(root_done, 1)
                act.wait_ge(out_ready, b + 1)
                act.sem_inc(act_go, 1)
                act.dma_start(out[bass.ds(b + DENSE_TILES, 1), :, :].rearrange("o p n -> (o p) n"), acc[:, 1, :]).then_inc(out_kept, 16)
            for t in range(DENSE_TILES):
                act.wait_ge(h3_ready, BLOCKS + t + 2)
                nc.scalar.activation(ring[:, DENSE_TILES, :], sums[:, t, :], ACT.Square, accum_out=col[:, 9:10])
                act.drain()
                nc.scalar.activation(col[:, 10:11], col[:, 9:10], ACT.Sqrt, bias=eps, scale=1.0 / D).then_inc(root_done, 1)
                act.wait_ge(out_ready, BLOCKS + t + 1)
                act.dma_start(out[t, :, :], ring[:, t, :]).then_inc(out_kept, 16)
            act.wait_ge(out_kept, 16 * TILES)

        @block.vector
        def _(dve):
            nc.vector.memset(ident[:], 1.0).then_inc(const_dve, 1)
            nc.vector.memset(ones[:], 1.0).then_inc(const_dve, 1)
            nc.vector.memset(eps, EPS).then_inc(const_dve, 1)
            dve.sem_inc(dve_emptied, per_half["dve"])
            dve.sem_inc(rows_used, RING)
            dve.sem_inc(s_used, 1)
            dve.sem_inc(h3_ready, 1)
            dve.sem_inc(w_ready, 2)
            dve.sem_inc(o_added, 4)
            dve.wait_ge(const_in, 80)
            def rank_keys(q):
                four = [(hp, ranking[:, hp * KEYS:(hp + 1) * KEYS], work[:, i * KEYS:(i + 1) * KEYS])
                        for i, hp in enumerate(range(4 * q, 4 * q + 4))]
                for hp, s, _ in four:
                    nc.vector.max(tops[:, hp, 0:8], s)
                dve.drain()
                for hp, s, rest in four:
                    nc.vector.max_index(topi[:, hp, 0:8], tops[:, hp, 0:8], s)
                    nc.vector.match_replace(rest, tops[:, hp, 0:8], s, LOWEST)
                dve.drain()
                for hp, _, rest in four:
                    nc.vector.max(tops[:, hp, 8:16], rest)
                dve.drain()
                for hp, _, rest in four:
                    nc.vector.max_index(topi[:, hp, 8:16], tops[:, hp, 8:16], rest)
                dve.drain()

            def rank_pairs(q):
                n = TOPK * TOPK
                cand, rest, hot = ranking[:, 0:2 * n], ranking[:, 2 * n:4 * n], ranking[:, 4 * n:8 * n]
                two = [(2 * q + i, cand[:, i * n:(i + 1) * n], rest[:, i * n:(i + 1) * n]) for i in range(2)]
                for hd, c, _ in two:
                    nc.vector.tensor_tensor(c.rearrange("p (a b) -> p a b", a=TOPK),
                                            tops[:, 2 * hd, :].unsqueeze(2).to_broadcast([P, TOPK, TOPK]),
                                            tops[:, 2 * hd + 1, :].unsqueeze(1).to_broadcast([P, TOPK, TOPK]), ALU.add)
                dve.drain()
                for hd, c, _ in two:
                    nc.vector.max(best[:, hd, 0:8], c)
                dve.drain()
                for hd, c, left in two:
                    nc.vector.max_index(pos[:, hd, 0:8], best[:, hd, 0:8], c)
                    nc.vector.match_replace(left, best[:, hd, 0:8], c, LOWEST)
                dve.drain()
                for hd, _, left in two:
                    nc.vector.max(best[:, hd, 8:16], left)
                dve.drain()
                for hd, _, left in two:
                    nc.vector.max_index(pos[:, hd, 8:16], best[:, hd, 8:16], left)
                dve.drain()
                both = pos[:, 2 * q:2 * q + 2, :]
                nc.vector.tensor_scalar(digit[:, :, 0, :], both, 4, None, ALU.logical_shift_right)
                nc.vector.tensor_scalar(digit[:, :, 1, :], both, TOPK - 1, None, ALU.bitwise_and)
                dve.drain()
                hot = hot.rearrange("p (h k a) -> p h k a", h=4, k=TOPK)
                nc.vector.tensor_tensor(hot, digit[:].rearrange("p h s k -> p (h s) k").unsqueeze(3).to_broadcast([P, 4, TOPK, TOPK]),
                                        iota[:, 0:TOPK].unsqueeze(1).unsqueeze(1).to_broadcast([P, 4, TOPK, TOPK]), ALU.is_equal)
                dve.drain()
                nc.vector.tensor_tensor(hot, hot, topi[:, 4 * q:4 * q + 4, :].unsqueeze(2).to_broadcast([P, 4, TOPK, TOPK]), ALU.mult)
                dve.drain()
                nc.vector.tensor_reduce(half_i[:, :, 2 * q * TOPK:(2 * q + 2) * TOPK].rearrange("p s (h k) -> p h s k", h=2),
                                        hot.rearrange("p (h s) k a -> p h s k a", s=2), AX.X, ALU.add)
                dve.drain()

            def keep_dense(t):
                nc.vector.tensor_copy(route[:, 0:2, t, :], half_i[:])
                last = nc.vector.tensor_tensor(route[:, 2, t, :].rearrange("p (h k) -> p h k", h=HEADS), best[:],
                                               best[:, :, 0:1].to_broadcast([P, HEADS, TOPK]), ALU.subtract)
                if t == DENSE_TILES - 1:
                    last.then_inc(d_shifted, 1)
                dve.drain()
                dve.sem_inc(s_used, 1)

            def rank_dense(t):
                dve.wait_ge(s_loaded, 16 * t + 16)
                for q in range(4):
                    rank_keys(q)
                for q in range(4):
                    rank_pairs(q)
                keep_dense(t)

            def mixers(h):
                def act_has(kind, i):
                    _, until = emptied_until(position[kind, i])
                    dve.wait_ge(act_emptied, (h + 1) * per_half["act"] + until)

                act_has("sumsq", 0)
                nc.vector.reciprocal(rstd[:, 0:COLS], std[:, 0:COLS])
                dve.drain()
                for k in range(KD):
                    nc.vector.scalar_tensor_tensor(out=xnT[:, k, :], in0=xnT[:, k, :], scalar=g_mix[:, k:k + 1],
                                                   in1=rstd[:, 0:COLS], op0=ALU.mult, op1=ALU.mult).then_inc(xn_ready, 1)
                if h == 1:
                    rank_dense(0)
                for g in range(NG):
                    act_has("proj", g)
                    a = proj[:, g, :]
                    src, width = a, 1
                    for r in range(g + 1):
                        dst = tA if r % 2 == 0 else tB
                        nc.vector.tensor_tensor(dst[:, 2 * width - 1:COLS], src[:, 2 * width - 1:COLS],
                                                src[:, width - 1:COLS - width], ALU.add)
                        dve.drain()
                        src, width = dst, 2 * width
                    nc.vector.scalar_tensor_tensor(out=yT[:, g, :], in0=src[:, META:COLS], scalar=1.0 / width,
                                                   in1=a[:, META:COLS], op0=ALU.mult, op1=ALU.subtract).then_inc(pooled, 1)
                    dve.drain()
                if h == 1:
                    dve.wait_ge(s_loaded, 32)
                    for q in range(4):
                        rank_keys(q)
                for g in range(NG):
                    act_has("proj", 12 + g)
                    b_gate, c_gate, val = (proj[:, 4 * q + g, :] for q in (1, 2, 3))
                    nc.vector.tensor_tensor(c_gate, c_gate, val, ALU.mult)
                    dve.drain()
                    nc.vector.tensor_scalar(tA[:, META:COLS], c_gate[:, META - 2:COLS - 2], convw[:, 0, g:g + 1], None, ALU.mult)
                    dve.drain()
                    nc.vector.scalar_tensor_tensor(out=tB[:, META:COLS], in0=c_gate[:, META - 1:COLS - 1], scalar=convw[:, 1, g:g + 1],
                                                   in1=tA[:, META:COLS], op0=ALU.mult, op1=ALU.add)
                    dve.drain()
                    nc.vector.scalar_tensor_tensor(out=tA[:, META:COLS], in0=c_gate[:, META:COLS], scalar=convw[:, 2, g:g + 1],
                                                   in1=tB[:, META:COLS], op0=ALU.mult, op1=ALU.add)
                    dve.drain()
                    nc.vector.tensor_tensor(val[:, 0:HT], b_gate[:, META:COLS], tA[:, META:COLS], ALU.mult).then_inc(conv_done, 1)
                act_has("ynorm", 0)
                nc.vector.reciprocal(rstd, std)
                dve.drain()
                for k in range(KD):
                    src = proj[:, k if k < NG else 8 + k, 0:HT]
                    r = rstd[:, 0:HT] if k < NG else rstd[:, HT:2 * HT]
                    nc.vector.scalar_tensor_tensor(out=yT[:, k, :], in0=src, scalar=g_ab[:, k:k + 1], in1=r,
                                                   op0=ALU.mult, op1=ALU.mult).then_inc(y_ready, 1)
                for t in range(TT):
                    n = position["outp", t]
                    dve.wait_ge(pe_step, h * NSTEP + n + 2)
                    dve.wait_ge(xt_loaded[t % 2], h * 32 + 16 * (t // 2) + 16)
                    if t >= 2:
                        dve.wait_ge(kept[t % 2], h * 64 + 32 * (t // 2))
                    nc.vector.tensor_tensor(h2b[:, t % 2, :], psum[:, n % PAIRS, :], xt[:, t % 2, :], ALU.add).then_inc(dve_emptied, 1)
                    dve.wait_ge(std_ready, h * TT + t + 1)
                    nc.vector.reciprocal(col[:, 11 + t % 2:12 + t % 2], col[:, 5 + t:6 + t])
                    dve.drain()
                    if t >= 2:
                        dve.wait_ge(pe_step, h * NSTEP + position["turn", t - 2] + 2)
                    nc.vector.scalar_tensor_tensor(out=xfb[:, t % 2, :], in0=h2b[:, t % 2, :], scalar=col[:, 11 + t % 2:12 + t % 2],
                                                   in1=g_ffn, op0=ALU.mult, op1=ALU.mult).then_inc(xf_ready, 1)
                    if h == 1:
                        rank_pairs(t)
                if h == 1:
                    for t in range(1, DENSE_TILES):
                        keep_dense(t) if t == 1 else rank_dense(t)

            for h in range(HALVES):
                mixers(h)

            scores_d = route[:, 2, :, :].rearrange("p t (h k) -> p (t h) k", h=HEADS)
            dve.wait_ge(d_exped, 1)
            nc.vector.tensor_reduce(gsum[:, 0, :], scores_d, AX.X, ALU.add)
            dve.drain()
            nc.vector.reciprocal(gsum[:, 1, :], gsum[:, 0, :])
            dve.drain()
            nc.vector.tensor_tensor(scores_d, scores_d, gsum[:, 1, :].unsqueeze(2).to_broadcast([P, DENSE_TILES * HEADS, TOPK]),
                                    ALU.mult).then_inc(d_gates, 1)

            def hand_over():
                nc.vector.tensor_tensor(weight[:].rearrange("p (h k) -> p h k", h=HEADS), best[:],
                                        best[:, :, 0:1].to_broadcast([P, HEADS, TOPK]), ALU.subtract).then_inc(shifted, 1)
                nc.vector.scalar_tensor_tensor(out=idx[:], in0=half_i[:, 0, :], scalar=float(KEYS), in1=half_i[:, 1, :],
                                               op0=ALU.mult, op1=ALU.add).then_inc(routed, 1)

            def normalise(b):
                dve.wait_ge(exped, b + 1)
                nc.vector.tensor_reduce(gsum[:, 0, 0:HEADS], gexp[:], AX.X, ALU.add)
                dve.drain()
                nc.vector.reciprocal(gsum[:, 1, 0:HEADS], gsum[:, 0, 0:HEADS])
                dve.drain()
                nc.vector.tensor_tensor(gates[:].rearrange("p (h k) -> p h k", h=HEADS), gexp[:],
                                        gsum[:, 1, 0:HEADS].unsqueeze(2).to_broadcast([P, HEADS, TOPK]), ALU.mult)
                dve.drain()

            def dense_item(b, item):
                g, m = item // (2 * GJ), item % (2 * GJ)
                if m < GJ:
                    if m == 0:
                        dve.wait_ge(g_in, b * (16 * PER_BLOCK) + 16 * g + 16)
                    dve.wait_ge(act_ready, b * (GJ * PER_BLOCK) + g * GJ + m + 3)
                    nc.vector.tensor_tensor(gated[:, m, :], acts[:, m % 2, :],
                                            gtab.rearrange("p (t j) -> p t j", j=GJ)[:, :, m], ALU.mult).then_inc(w_ready, 1)
                else:
                    n = m - GJ
                    dve.wait_ge(o_full, b * (SUMS * PER_BLOCK) + g * SUMS + n + 2)
                    piece = sums[:, n // 2, (n % 2) * HT:(n % 2 + 1) * HT]
                    nc.vector.tensor_tensor(piece, piece, o_bank[n % 4], ALU.add).then_inc(o_added, 1)

            def expert_block(b, rank_next):
                normalise(b)
                dve.wait_ge(xf_in, b * 16 + 16)
                for n in range(2 * HK):
                    k = n % HK
                    if n == HK:
                        dve.wait_ge(gelu_done, b + 1)
                        nc.vector.tensor_tensor(weight[:], gelu[:], gates[:], ALU.mult)
                        dve.drain()
                    row = ring[:, n % RING, :]
                    dve.wait_ge(row_in[n % RING], b * (16 * 2 * HK // RING) + 16 * (n // RING) + 16)
                    dve.wait_ge(rows_used, b * (2 * HK) + n + RING - 1)
                    if n < HK:
                        nc.vector.tensor_tensor_reduce(out=junk[:, n % 2, :], in0=row, in1=xf, scale=1.0, scalar=0.0,
                                                       op0=ALU.mult, op1=ALU.add, accum_out=dots[:, k:k + 1]).then_inc(rows_used, 1)
                    elif k < 2:
                        nc.vector.tensor_scalar(acc[:, k, :], row, weight[:, k:k + 1], None, ALU.mult).then_inc(rows_used, 1)
                    else:
                        nc.vector.scalar_tensor_tensor(out=acc[:, k % 2, :], in0=row, scalar=weight[:, k:k + 1], in1=acc[:, k % 2, :],
                                                       op0=ALU.mult, op1=ALU.add).then_inc(rows_used, 1)
                    if n % EVERY == EVERY - 1:
                        dense_item(b, n // EVERY)
                    if rank_next:
                        if n == 0:
                            dve.wait_ge(s_loaded, b * 16 + 16 * (DENSE_TILES + 2))
                        if n < HK and k % 32 == 31:
                            rank_keys(k // 32)
                        if n >= HK and k % 32 == 31:
                            rank_pairs(k // 32)
                dve.drain()
                nc.vector.tensor_tensor(acc[:, 0, :], acc[:, 0, :], acc[:, 1, :], ALU.add)
                if rank_next:
                    dve.sem_inc(s_used, 1)
                    hand_over()
                dve.drain()
                dve.wait_ge(h2_in, b * 16 + 16)
                nc.vector.tensor_tensor(acc[:, 0, :], acc[:, 0, :], h2, ALU.add).then_inc(h3_ready, 1)
                dve.wait_ge(root_done, b + 1)
                nc.vector.reciprocal(col[:, 13:14], col[:, 10:11])
                dve.drain()
                nc.vector.scalar_tensor_tensor(out=acc[:, 1, :], in0=acc[:, 0, :], scalar=col[:, 13:14], in1=g_final[:],
                                               op0=ALU.mult, op1=ALU.mult).then_inc(out_ready, 1)
                dve.wait_ge(out_kept, b * 16 + 16)

            dve.wait_ge(s_loaded, 16 * (DENSE_TILES + 1))
            for q in range(4):
                rank_keys(q)
            for q in range(4):
                rank_pairs(q)
            dve.sem_inc(s_used, 1)
            dve.wait_ge(mixers_done, 1)
            hand_over()

            dve.wait_ge(turned_out, DENSE_TILES)
            with dve.Fori(0, HT // (4 * HOTS)) as it:
                for c in range(4):
                    dve.wait_ge(table_full, it * 8 + 2 * c + 2)
                    dve.sem_inc(dve_go, 1)
                    for side in range(2):
                        last = nc.vector.tensor_tensor(hots[:, c % 2, side], iota[:].unsqueeze(1).to_broadcast([P, HOTS, KEYS]),
                                                       keysT[:, side, bass.ds((it * 4 + c) * HOTS, HOTS)].unsqueeze(2).to_broadcast([P, HOTS, KEYS]),
                                                       ALU.is_equal)
                    last.then_inc(hot_ready, 1)
            nc.vector.memset(sums.rearrange("p t d -> p (t d)"), 0.0)
            dve.drain()
            with dve.Fori(0, BLOCKS - 1) as b:
                expert_block(b, True)
            expert_block(BLOCKS - 1, False)
            dve.wait_ge(d_h2_in, 16)
            for t in range(DENSE_TILES):
                nc.vector.tensor_tensor(sums[:, t, :], sums[:, t, :], ring[:, t, :], ALU.add).then_inc(h3_ready, 1)
                dve.wait_ge(root_done, BLOCKS + t + 1)
                nc.vector.reciprocal(col[:, 13:14], col[:, 10:11])
                dve.drain()
                nc.vector.scalar_tensor_tensor(out=ring[:, t, :], in0=sums[:, t, :], scalar=col[:, 13:14], in1=g_final[:],
                                               op0=ALU.mult, op1=ALU.mult).then_inc(out_ready, 1)


def kernel(x, meta_tokens, norm_mix_g, w_in, pool_w, pool_scale, conv_w, norm_a_g, norm_b_g, w_out, norm_ffn_g,
           w_query, sub_keys, expert_u, expert_v, norm_final_g):
    import concourse.bacc as bacc
    from concourse.bass_utils import run_bass_kernel_spmd

    a = lambda v: np.asarray(v)
    tiles_first = lambda w: np.ascontiguousarray(w.reshape(KD, P, -1).transpose(1, 0, 2))
    per_partition = lambda v: v.reshape(-1, P).T
    x2 = a(x)[0]
    h = np.concatenate([a(meta_tokens), x2], axis=0)
    small = np.concatenate([per_partition(a(norm_mix_g)[0]), per_partition(a(pool_scale)[0]),
                            per_partition(a(conv_w)[0].reshape(-1)), per_partition(a(norm_a_g)[0]),
                            per_partition(a(norm_b_g)[0])], axis=1)
    rows_g = np.concatenate([a(norm_ffn_g)[0], a(norm_final_g)])[None, :].repeat(P, axis=0)
    arrays = {
        "hT": tiles_first(h.T),
        "x": x2.reshape(TILES, P, D),
        "w_in": tiles_first(a(w_in)[0]),
        "w_out": tiles_first(a(w_out)[0]),
        "w_query": tiles_first(a(w_query)[0]),
        "sub_keys": a(sub_keys)[0].transpose(3, 0, 1, 2).reshape(P, HP * KEYS),
        "pool_w": a(pool_w)[0].transpose(1, 0, 2).reshape(P, NG * P),
        "small": small,
        "rows_g": rows_g,
        "expert_u": a(expert_u)[0],
        "expert_v": a(expert_v)[0],
        "uT": a(expert_u)[0].reshape(KEYS, KEYS, KD, P).transpose(1, 3, 2, 0).reshape(KEYS, P, D),
    }
    arrays = {f"in_{n}": np.ascontiguousarray(v) for n, v in arrays.items()}
    nc = bacc.Bacc("TRN2", target_bir_lowering=False, num_devices=1)
    args = [nc.dram_tensor(n, v.shape, mybir.dt.from_np(v.dtype), kind="ExternalInput").ap() for n, v in arrays.items()]
    result = nc.dram_tensor("out", (TILES, P, D), FP32, kind="ExternalOutput").ap()
    program(nc, *args, result)
    r = run_bass_kernel_spmd(nc, [arrays], core_ids=[0])
    return r.results[0]["out"].reshape(1, SEQ, D)
```

```python
import concourse.bass as bass
from concourse import mybir
from concourse.alu_op_type import AluOpType as ALU
from contextlib import ExitStack
import numpy as np

FP32 = mybir.dt.float32
U32 = mybir.dt.uint32
BF16 = mybir.dt.bfloat16
ACT = mybir.ActivationFunctionType
AX = mybir.AxisListType

P = 128
D = 1024
KD = D // P
SEQ, META = 1024, 16
HALVES = 2
HT = SEQ // HALVES
TT = HT // P
TILES = SEQ // P
COLS = HT + META
HB = COLS // 2
CT = 16
NG = 4
HEADS, KEYS, TOPK = 8, 128, 16
HP = 2 * HEADS
HK = HEADS * TOPK
SLOTW = 512
EPS = 1e-6
LOWEST = -3.0e38
DENSE_TILES = TT
BLOCKS = TILES - DENSE_TILES
RING = 8
GJ = 4
GROUPS = KEYS // GJ
TURNS = BLOCKS - 1
PER_TURN = 9
LAST_GROUPS = GROUPS - TURNS * PER_TURN
SUMS = 2 * DENSE_TILES
GBUFS = 3
assert PER_TURN % GBUFS == 0 and 0 < LAST_GROUPS
USLOTS = GJ
HOTS = 8
HOTBUFS = 4
HOT_TURNS = HT // (HOTBUFS * HOTS)
RANK_TURNS = 2
HOT_ROWS = RING // HOTBUFS
assert HOT_ROWS * HOTBUFS == RING and RING * HOT_TURNS == HK
CHUNK = 32


def program(nc, hT, x, w_in, w_out, w_query, sub_keys, pool_w, small, rows_g, expert_u, expert_v, uT, out):
    h2_d = nc.dram_tensor("h2_scratch", (TILES, P, D), FP32, kind="Internal").ap()
    xf_d = nc.dram_tensor("xf_scratch", (TILES, P, D), FP32, kind="Internal").ap()
    s_d = nc.dram_tensor("score_scratch", (TILES, P, HP * KEYS), FP32, kind="Internal").ap()
    xfT_d = nc.dram_tensor("xfT_scratch", (P, KD, HT), FP32, kind="Internal").ap()
    g_d = nc.dram_tensor("gate_tables", (GROUPS, P, HT * GJ), FP32, kind="Internal").ap()
    v_rows = expert_v.rearrange("(i j) d -> i (j d)", j=KEYS)

    steps = ([("sumsq", 0, "act")] + [("proj", c, "act") for c in range(CT)]
             + [("pool", i, "act") for i in range(2)] + [("ynorm", 0, "act")]
             + [("outp", t, "dve") for t in range(TT)] + [("turn", t, "act") for t in range(TT)]
             + [("query", c, "act") for c in range(CT // 2)] + [("score", i, "act") for i in range(2 * TT)])
    NSTEP = len(steps)
    PAIRS = 4
    assert NSTEP % PAIRS == 0
    position = {(kind, i): n for n, (kind, i, _) in enumerate(steps)}
    per_half = {e: sum(s[2] == e for s in steps) for e in ("act", "dve")}

    def emptied_until(n):
        e = steps[n][2]
        return e, sum(s[2] == e for s in steps[:n + 1])

    def gated_tiles(items):
        return sum(kind == "gate" for kind, _, _ in items)

    def items_of(groups, last):
        return [item for i in range(groups)
                for item in [("gate", i + 1, m) for m in range(GJ) if not (last and i == groups - 1)] + [("sum", i, n) for n in range(SUMS)]]

    turn_items, last_items = items_of(PER_TURN, False), items_of(LAST_GROUPS, True)

    def spread(items, rows):
        cost = np.cumsum([2 if kind == "gate" else 1 for kind, _, _ in items])
        return [int(np.sum(cost * rows <= cost[-1] * (n + 1))) for n in range(rows)]

    turn_spread, last_spread = spread(turn_items, 2 * HK), spread(last_items, HK - RING) + [len(last_items)] * RING

    LOADS = 10

    ctx = ExitStack()
    with ctx:
        def sb(name, shape, dt=FP32):
            return ctx.enter_context(nc.sbuf_tensor(name, shape, dt))

        def sem(name):
            return ctx.enter_context(nc.semaphore(name))

        SCRATCH = 8 * TOPK * TOPK
        ARENA = 40 * D + SCRATCH
        arena = sb("arena", [P, ARENA])
        views = {}

        def place(names):
            o = 0
            for name, shape in names:
                n = int(np.prod(shape))
                v = arena[:, o:o + n]
                if len(shape) > 1:
                    v = v.rearrange("p (a b) -> p a b", a=shape[0])
                views[name] = v
                o += n
            assert o <= ARENA, o

        place([("wslot0", (KD, SLOTW)), ("wslot1", (KD, SLOTW)), ("yT", (KD, HT)), ("tA", (COLS,)), ("tB", (COLS,)),
               ("xnT", (KD, COLS)), ("proj", (CT, COLS)), ("std", (2 * HT,)), ("rstd", (2 * HT,)), ("xt", (2, D)), ("h2b", (2, D)),
               ("xfb", (2, D)), ("squared", (D,)), ("scores", (HP * KEYS,)), ("skT", (HP * KEYS,)), ("poolw", (NG, P)),
               ("g_ffn", (D,))])
        place([("before", (2 * KD * SLOTW,)), ("xsq", (KD, COLS))])
        place([("uslot", (USLOTS, D)), ("vrows", (GJ, D)), ("gtab", (HT * GJ,)), ("gated", (GBUFS * GJ, HT)),
               ("sums", (DENSE_TILES, D)), ("xfT", (KD, HT)), ("acts", (GJ, HT)), ("ring", (RING, D)), ("xf", (D,)),
               ("h2", (D,)), ("acc", (2, D)), ("junk32", (D,)), ("junk_a", (D,))])
        place([("before", (USLOTS * D,)), ("tables", (2 * KEYS * CHUNK,)), ("hots", (HOTBUFS * 2 * HOTS * KEYS,))])
        place([("before", (ARENA - SCRATCH,)), ("pair_scratch", (SCRATCH,))])
        wslot = [views["wslot0"], views["wslot1"]]
        yT, xnT, proj, tA, tB, std, rstd, xt, h2b, xfb, squared, scores, skT, poolw, g_ffn = (views[n] for n in (
            "yT", "xnT", "proj", "tA", "tB", "std", "rstd", "xt", "h2b", "xfb", "squared", "scores", "skT", "poolw", "g_ffn"))
        uslot, vrows, gtab, gated, sums, xfT, acts, ring, xf, h2, acc = (views[n] for n in (
            "uslot", "vrows", "gtab", "gated", "sums", "xfT", "acts", "ring", "xf", "h2", "acc"))
        xsq, junk_a = views["xsq"], views["junk_a"]
        junk = views["junk32"].bitcast(BF16).rearrange("p (r d) -> p r d", r=2)
        hots = views["hots"].rearrange("p (c s t j) -> p c s t j", c=HOTBUFS, s=2, j=KEYS)
        tables = views["tables"].rearrange("p (c g t j) -> p c g t j", c=2, g=GROUPS, t=CHUNK)
        ranking = sb("ranking", [P, HP * KEYS])
        work = sb("work", [P, 4 * KEYS])
        col = sb("col", [P, 16])
        smalls = sb("smalls", [P, 32])
        g_final = sb("g_final", [P, D])
        ident = sb("ident", [P, P])
        ones = sb("ones", [P, P])
        iota = sb("iota", [P, KEYS])
        tops = sb("tops", [P, HP, TOPK])
        topi = sb("topi", [P, HP, TOPK], U32)
        best = sb("best", [P, HEADS, TOPK])
        pos = sb("pos", [P, HEADS, TOPK], U32)
        digit = sb("digit", [P, 2, 2, TOPK], U32)
        half_i = sb("half_i", [P, 2, HK])
        route = sb("route", [P, 3, DENSE_TILES, HK])
        routeT = sb("routeT", [P, 3, DENSE_TILES, P])
        keysT = routeT[:].rearrange("p m t k -> p m (t k)")
        gexp = sb("gexp", [P, HEADS, TOPK])
        gsum = sb("gsum", [P, 2, DENSE_TILES * HEADS])
        idx_u = sb("idx_u", [P, HK], U32)
        idx_now = sb("idx_now", [P, RING], U32)
        idx_v = sb("idx_v", [P, HK], U32)
        gates = sb("gates", [P, HK])
        dots = sb("dots", [P, HK])
        dots_now = sb("dots_now", [P, RING])
        gelu = sb("gelu", [P, HK])
        weight = sb("weight", [P, HK])
        psum = ctx.enter_context(nc.psum_tensor("pairs", [P, PAIRS, 2 * HT], FP32))
        bank = [psum[:, n // 2, (n % 2) * HT:(n % 2 + 1) * HT] for n in range(8)]
        s_bank, o_bank, g_bank = bank[0:4], bank[4:8], bank[0:4]

        g_mix, pscale = smalls[:, 0:8], smalls[:, 8:12]
        convw = smalls[:, 12:24].rearrange("p (w c) -> p w c", w=3)
        g_ab = smalls[:, 24:32]
        eps = col[:, 0:1]

        const_in = sem("const_in")
        const_dve = sem("const_dve")
        const_pool = sem("const_pool")
        w_loaded = [sem(f"w_loaded{i}") for i in range(2)]
        w_used = sem("w_used")
        xT_loaded = [sem(f"xT_loaded{i}") for i in range(2)]
        xt_loaded = [sem(f"xt_loaded{i}") for i in range(2)]
        x_squared = sem("x_squared")
        squares = sem("squares")
        pe_step = sem("pe_step")
        act_emptied = sem("act_emptied")
        dve_emptied = sem("dve_emptied")
        emptied = {"act": act_emptied, "dve": dve_emptied}
        std_ready = sem("std_ready")
        xn_ready = sem("xn_ready")
        pooled = sem("pooled")
        conv_done = sem("conv_done")
        y_ready = sem("y_ready")
        xf_ready = sem("xf_ready")
        kept = [sem(f"kept{i}") for i in range(2)]
        xfT_kept = sem("xfT_kept")
        scores_kept = sem("scores_kept")
        s_loaded = sem("s_loaded")
        s_used = sem("s_used")
        xf_in = sem("xf_in")
        h2_in = sem("h2_in")
        routed_u = sem("routed_u")
        routed_v = sem("routed_v")
        shifted = sem("shifted")
        exped = sem("exped")
        row_in = [sem(f"row_in{i}") for i in range(RING)]
        rows_used = sem("rows_used")
        pool_go = sem("pool_go")
        sp_go = sem("sp_go")
        act_go = sem("act_go")
        pe_go = sem("pe_go")
        dve_go = sem("dve_go")
        idx_moved = sem("idx_moved")
        dots_kept = sem("dots_kept")
        gelu_done = sem("gelu_done")
        h3_ready = sem("h3_ready")
        root_done = sem("root_done")
        out_ready = sem("out_ready")
        out_kept = sem("out_kept")
        mixers_done = sem("mixers_done")
        d_shifted = sem("d_shifted")
        d_exped = sem("d_exped")
        d_gates = sem("d_gates")
        turned = sem("turned")
        turned_out = sem("turned_out")
        hot_ready = sem("hot_ready")
        hot_first = sem("hot_first")
        hot_gated = sem("hot_gated")
        table_full = sem("table_full")
        table_out = sem("table_out")
        table_kept = [sem(f"table_kept{i}") for i in range(2)]
        xfT_in = sem("xfT_in")
        u_in = [sem(f"u_in{i}") for i in range(USLOTS)]
        v_in = sem("v_in")
        g_in = sem("g_in")
        s_full = sem("s_full")
        act_ready = sem("act_ready")
        w_ready = sem("w_ready")
        o_full = sem("o_full")
        o_added = sem("o_added")
        d_h2_in = sem("d_h2_in")

        block = ctx.enter_context(nc.Block())

        @block.sync
        def _(sp):
            for i in range(2):
                sp.dma_start(xnT[:, 4 * i:4 * i + 4, :], hT[:, 4 * i:4 * i + 4, 0:COLS]).then_inc(xT_loaded[i], 16)
            sp.dma_start(smalls[:], small).then_inc(const_in, 16)
            sp.dma_start(skT, sub_keys).then_inc(const_in, 16)
            sp.dma_start(poolw.rearrange("p g n -> p (g n)"), pool_w).then_inc(const_in, 16)
            sp.dma_start(g_ffn, rows_g[:, 0:D]).then_inc(const_in, 16)
            sp.dma_start(g_final[:], rows_g[:, D:2 * D]).then_inc(const_in, 16)
            for h in range(HALVES):
                for n in range(LOADS):
                    if n == 6:
                        for t in range(TT):
                            sp.wait_ge(xf_ready, h * TT + t + 1)
                            row = bass.ds(h * TT + t, 1)
                            sp.dma_start(h2_d[row, :, :].rearrange("o p n -> (o p) n"), h2b[:, t % 2, :]).then_inc(kept[t % 2], 16)
                            sp.dma_start(xf_d[row, :, :].rearrange("o p n -> (o p) n"), xfb[:, t % 2, :]).then_inc(kept[t % 2], 16)
                        if h == 0:
                            _, until = emptied_until(position["turn", TT - 1])
                            sp.wait_ge(act_emptied, (h + 1) * per_half["act"] + until)
                            sp.dma_start(xfT_d, xnT[:, :, 0:HT]).then_inc(xfT_kept, 16)
                    sp.wait_ge(w_used, h * LOADS + n + 1)
                    src = w_in if n < 4 else w_out if n < 6 else w_query
                    c = (n if n < 4 else n - 4 if n < 6 else n - 6) * SLOTW
                    sp.dma_start(wslot[n % 2], src[:, :, c:c + SLOTW]).then_inc(w_loaded[n % 2], 16)
                if h + 1 < HALVES:
                    sp.wait_ge(pe_step, h * NSTEP + position["query", CT // 2 - 1] + 2)
                    sp.wait_ge(xfT_kept, 16)
                    for i in range(2):
                        sp.dma_start(xnT[:, 4 * i:4 * i + 4, :],
                                     hT[:, 4 * i:4 * i + 4, (h + 1) * HT:(h + 1) * HT + COLS]).then_inc(xT_loaded[i], 16)
                for t in range(TT):
                    _, until = emptied_until(position["score", 2 * t + 1])
                    sp.wait_ge(act_emptied, (h + 1) * per_half["act"] + until)
                    sp.dma_start(s_d[bass.ds(h * TT + t, 1), :, :].rearrange("o p n -> (o p) n"), scores[:]).then_inc(scores_kept, 16)
                sp.wait_ge(scores_kept, h * (16 * TT) + 16 * TT)
                sp.wait_ge(kept[0], h * 64 + 64)
                sp.wait_ge(kept[1], h * 64 + 64)
            sp.sem_inc(mixers_done, 1)

            def load_u(g, j):
                sp.wait_ge(s_full, g * GJ + j + 1)
                sp.sem_inc(sp_go, 1)
                sp.dma_start(uslot[:, j % USLOTS, :], uT[bass.ds(g * GJ + j, 1), :, :].rearrange("o p n -> (o p) n")).then_inc(u_in[j % USLOTS], 16)

            def load_v(g):
                sp.wait_ge(o_full, g * SUMS + 1)
                sp.sem_inc(sp_go, 1)
                sp.dma_start(vrows.rearrange("p j d -> p (j d)"), v_rows[:, bass.ds(g * (GJ * D), GJ * D)]).then_inc(v_in, 16)

            def load_gates(g):
                sp.wait_ge(w_ready, g * GJ + GJ)
                sp.sem_inc(sp_go, 1)
                sp.dma_start(gtab, g_d[bass.ds(g, 1), :, :].rearrange("o p n -> (o p) n")).then_inc(g_in, 16)

            sp.dma_start(xfT, xfT_d).then_inc(xfT_in, 16)
            for j in range(GJ):
                load_u(0, j)
            with sp.Fori(0, HT // (2 * CHUNK)) as it:
                for c in range(2):
                    sp.wait_ge(table_out, it * (CHUNK // 2) + (c + 1) * (CHUNK // 4) + 4)
                    sp.sem_inc(sp_go, 1)
                    sp.dma_start(g_d[:, :, bass.ds((it * 2 + c) * (CHUNK * GJ), CHUNK * GJ)].rearrange("g p n -> p g n"),
                                 tables[:, c].rearrange("p g t j -> p g (t j)")).then_inc(table_kept[c], 16)
            sp.wait_ge(table_kept[0], 16 * HT // (2 * CHUNK))
            sp.wait_ge(table_kept[1], 16 * HT // (2 * CHUNK))
            load_gates(0)
            load_v(0)
            sp.wait_ge(table_full, HT // 4 + 2 * HOTBUFS)
            sp.dma_start(sums, h2_d[0:DENSE_TILES, :, :].rearrange("t p d -> p t d")).then_inc(d_h2_in, 16)
            for j in range(GJ):
                load_u(1, j)
            load_gates(1)
            with sp.Fori(0, GROUPS - 2) as g:
                for j in range(GJ):
                    load_u(g + 2, j)
                load_gates(g + 2)
                load_v(g + 1)
            load_v(GROUPS - 1)
            for t in range(DENSE_TILES):
                sp.wait_ge(out_ready, BLOCKS + t)
                sp.dma_start(out[t, :, :], sums[:, t, :]).then_inc(out_kept, 16)

        @block.gpsimd
        def _(pool):
            pool.wait_ge(const_dve, 1)
            nc.gpsimd.affine_select(out=ident[:], in_=ident[:], compare_op=ALU.is_equal, fill=0.0, base=0,
                                    pattern=[[-1, P]], channel_multiplier=1).then_inc(const_pool, 1)
            nc.gpsimd.iota(iota[:], [[1, KEYS]], base=0, channel_multiplier=0,
                           allow_small_or_imprecise_dtypes=True).then_inc(const_pool, 1)
            with pool.Fori(0, DENSE_TILES + 1) as t:
                pool.wait_ge(s_used, t + 1)
                pool.wait_ge(scores_kept, t * 16 + 16)
                pool.sem_inc(pool_go, 1)
                pool.dma_start(ranking[:], s_d[bass.ds(t, 1), :, :].rearrange("o p n -> (o p) n")).then_inc(s_loaded, 16)
            tile = lambda d, n: d[bass.ds(n + DENSE_TILES, 1), :, :].rearrange("o p n -> (o p) n")

            def gather(table, idx, r, k, slot):
                pool.wait_ge(rows_used, r + 1)
                pool.sem_inc(pool_go, 1)
                nc.gpsimd.indirect_dma_start(out=ring[:, slot, :], out_offset=None, in_=table,
                                             in_offset=bass.IndirectOffsetOnAxis(ap=idx[:, k:k + 1], axis=0)).then_inc(row_in[slot], 16)

            def hots_times_gates(it, rows):
                for c in range(HOTBUFS):
                    pool.wait_ge(hot_ready, it * HOTBUFS + c + 1)
                    pool.sem_inc(pool_go, 1)
                    nc.gpsimd.tensor_tensor(hots[:, c, 1], hots[:, c, 1],
                                            keysT[:, 2, bass.ds((it * HOTBUFS + c) * HOTS, HOTS)].unsqueeze(2).to_broadcast([P, HOTS, KEYS]),
                                            ALU.mult).then_inc(hot_gated, 1)
                    if rows:
                        slot = c * HOT_ROWS
                        r = it * RING + RING + slot
                        pool.wait_ge(rows_used, r + HOT_ROWS)
                        pool.sem_inc(pool_go, 1)
                        nc.gpsimd.tensor_copy(idx_now[:, slot:slot + HOT_ROWS], idx_u[:, bass.ds(r, HOT_ROWS)]).then_inc(idx_moved, 1)
                        pool.wait_ge(idx_moved, it * HOTBUFS + c + 1)
                        pool.sem_inc(pool_go, 1)
                        for i in range(HOT_ROWS):
                            gather(expert_u, idx_now, r + i, slot + i, slot + i)

            pool.wait_ge(routed_u, 1)
            pool.dma_start(xf, tile(xf_d, 0)).then_inc(xf_in, 16)
            for n in range(RING):
                gather(expert_u, idx_u, n, n, n)
            pool.wait_ge(turned_out, DENSE_TILES)
            for it in range(RANK_TURNS):
                hots_times_gates(it, True)
            pool.wait_ge(routed_u, 2)
            pool.wait_ge(s_used, DENSE_TILES + 2)
            pool.dma_start(ranking[:], tile(s_d, 1)).then_inc(s_loaded, 16)
            with pool.Fori(RANK_TURNS, HOT_TURNS - 1) as it:
                hots_times_gates(it, True)
            hots_times_gates(HOT_TURNS - 1, False)

            def gather_out(b, xf_next):
                pool.wait_ge(routed_v, b + 1)
                pool.sem_inc(pool_go, 1)
                for n in range(HK):
                    if n == RING and xf_next:
                        pool.wait_ge(rows_used, b * (2 * HK) + HK + RING)
                        pool.sem_inc(pool_go, 1)
                        pool.dma_start(xf, tile(xf_d, b + 1)).then_inc(xf_in, 16)
                    if n == HK // 2:
                        pool.wait_ge(h3_ready, b + 1)
                        pool.sem_inc(pool_go, 1)
                        pool.dma_start(h2, tile(h2_d, b)).then_inc(h2_in, 16)
                    gather(expert_v, idx_v, b * (2 * HK) + HK + n, n, n % RING)

            with pool.Fori(0, TURNS) as b:
                gather_out(b, True)
                pool.wait_ge(routed_u, b + 3)
                pool.sem_inc(pool_go, 1)
                for n in range(HK):
                    if n == RING:
                        pool.wait_ge(s_used, b + DENSE_TILES + 3)
                        pool.sem_inc(pool_go, 1)
                        pool.dma_start(ranking[:], s_d[bass.ds((b + 2) % BLOCKS + DENSE_TILES, 1), :, :].rearrange("o p n -> (o p) n")).then_inc(s_loaded, 16)
                    gather(expert_u, idx_u, b * (2 * HK) + 2 * HK + n, n, n % RING)
            gather_out(BLOCKS - 1, False)

        @block.tensor
        def _(pe):
            pe.sem_inc(w_used, 2)
            pe.sem_inc(pe_step, 1)
            pe.sem_inc(s_full, USLOTS)
            pe.sem_inc(table_full, 2 * HOTBUFS)
            pe.wait_ge(const_in, 80)
            pe.wait_ge(const_dve, 2)
            pe.wait_ge(const_pool, 2)
            with pe.Fori(0, HALVES) as h:
                def pair_free(n):
                    e, until = emptied_until((n - PAIRS) % NSTEP)
                    pe.wait_ge(emptied[e], (h + (n >= PAIRS)) * per_half[e] + until)

                load = [0]

                def next_slot():
                    n = load[0]
                    load[0] += 1
                    pe.wait_ge(w_loaded[n % 2], h * (16 * LOADS // 2) + 16 * (n // 2 + 1))
                    return wslot[n % 2]

                for n, (kind, i, _) in enumerate(steps):
                    pair = psum[:, n % PAIRS, :]
                    pair_free(n)
                    if kind == "sumsq":
                        for c in range(2):
                            for k in range(KD):
                                if c == 0:
                                    pe.wait_ge(x_squared, h * KD + k + 1)
                                last = nc.tensor.matmul(pair[:, c * HT:c * HT + HB], ones[:], xsq[:, k, c * HB:(c + 1) * HB],
                                                        start=(k == 0), stop=(k == KD - 1))
                    elif kind == "proj":
                        if i % 4 == 0:
                            w = next_slot()
                        for c in range(2):
                            for k in range(KD):
                                if i == 0 and c == 0:
                                    pe.wait_ge(xn_ready, h * KD + k + 1)
                                last = nc.tensor.matmul(pair[:, c * HT:c * HT + HB], w[:, k, (i % 4) * P:(i % 4 + 1) * P],
                                                        xnT[:, k, c * HB:(c + 1) * HB], start=(k == 0), stop=(k == KD - 1))
                        if i % 4 == 3:
                            pe.drain()
                            pe.sem_inc(w_used, 1)
                    elif kind == "pool":
                        for c in range(2):
                            pe.wait_ge(pooled, h * NG + 2 * i + c + 1)
                            last = nc.tensor.matmul(pair[:, c * HT:(c + 1) * HT], poolw[:, 2 * i + c, :], yT[:, 2 * i + c, :],
                                                    start=True, stop=True)
                    elif kind == "ynorm":
                        pe.wait_ge(squares, h + 1)
                        for c in range(2):
                            for k in range(NG):
                                last = nc.tensor.matmul(pair[:, c * HT:(c + 1) * HT], ones[:], xnT[:, c * NG + k, 0:HT],
                                                        start=(k == 0), stop=(k == NG - 1))
                    elif kind == "outp":
                        if i == 0:
                            wo = [next_slot(), next_slot()]
                        for c in range(2):
                            for k in range(KD):
                                if i == 0 and c == 0:
                                    pe.wait_ge(y_ready, h * KD + k + 1)
                                last = nc.tensor.matmul(pair[:, c * HT:(c + 1) * HT], yT[:, k, i * P:(i + 1) * P], wo[c][:, k, :],
                                                        start=(k == 0), stop=(k == KD - 1))
                        if i == TT - 1:
                            pe.drain()
                            pe.sem_inc(w_used, 2)
                    elif kind == "turn":
                        pe.wait_ge(xf_ready, h * TT + i + 1)
                        for k in range(KD):
                            last = nc.tensor.transpose(pair[:, k * P:(k + 1) * P], xfb[:, i % 2, k * P:(k + 1) * P], ident[:])
                    elif kind == "query":
                        if i == 0:
                            e, until = emptied_until(position["turn", TT - 1])
                            pe.wait_ge(emptied[e], (h + 1) * per_half[e] + until)
                        if i % 2 == 0:
                            w = next_slot()
                        for c in range(2):
                            m = (2 * i + c) % 4
                            for k in range(KD):
                                last = nc.tensor.matmul(pair[:, c * HT:(c + 1) * HT], w[:, k, m * P:(m + 1) * P], xnT[:, k, 0:HT],
                                                        start=(k == 0), stop=(k == KD - 1))
                        if i % 2 == 1:
                            pe.drain()
                            pe.sem_inc(w_used, 1)
                    elif kind == "score":
                        if i == 0:
                            e, until = emptied_until(position["query", CT // 2 - 1])
                            pe.wait_ge(emptied[e], (h + 1) * per_half[e] + until)
                        t, m = i // 2, i % 2
                        for c in range(HEADS):
                            hp = m * HEADS + c
                            last = nc.tensor.matmul(pair[:, c * KEYS:(c + 1) * KEYS], proj[:, hp, t * P:(t + 1) * P],
                                                    skT[:, hp * KEYS:(hp + 1) * KEYS], start=True, stop=True)
                    last.then_inc(pe_step, 1)

            pe.wait_ge(d_gates, 1)
            e, until = emptied_until(NSTEP - 1)
            pe.wait_ge(emptied[e], HALVES * per_half[e] + until)
            for t in range(DENSE_TILES):
                for m in range(3):
                    last = nc.tensor.transpose(bank[4 + t][:, m * P:(m + 1) * P], route[:, m, t, :], ident[:])
                last.then_inc(turned, 1)
            with pe.Fori(0, HT // (HOTBUFS * HOTS)) as it:
                for c in range(HOTBUFS):
                    pe.wait_ge(hot_gated, it * HOTBUFS + c + 1)
                    pe.wait_ge(hot_first, it * HOTBUFS + c + 1)
                    for m in range(2):
                        pe.wait_ge(table_out, it * (2 * HOTBUFS) + 2 * c + m + 1)
                        pe.sem_inc(pe_go, 1)
                        for q in range(4):
                            last = nc.tensor.matmul(g_bank[(2 * c + m) % 4][:, q * KEYS:(q + 1) * KEYS], hots[:, c, 0, 4 * m + q, :],
                                                    hots[:, c, 1, 4 * m + q, :], start=True, stop=True)
                        last.then_inc(table_full, 1)

            pe.sem_inc(o_full, 1)
            pe.wait_ge(xfT_in, 16)
            pe.wait_ge(table_out, HT // 4 + 4)

            def tiles_of(g):
                for j in range(GJ):
                    pe.wait_ge(u_in[j], g * 16 + 16)
                    pe.wait_ge(act_ready, g * GJ + j + 1)
                    pe.sem_inc(pe_go, 1)
                    for k in range(KD):
                        last = nc.tensor.matmul(s_bank[j], uslot[:, j, k * P:(k + 1) * P], xfT[:, k, :],
                                                start=(k == 0), stop=(k == KD - 1))
                    last.then_inc(s_full, 1)

            def pieces_of(g, buf):
                for n in range(SUMS):
                    t, half = n // 2, n % 2
                    pe.wait_ge(o_added, g * SUMS + n + 1)
                    pe.sem_inc(pe_go, 1)
                    for j in range(GJ):
                        if n == 0:
                            if j == 0:
                                pe.wait_ge(v_in, g * 16 + 16)
                            pe.wait_ge(w_ready, g * GJ + j + GJ + 1)
                            pe.sem_inc(pe_go, 1)
                        last = nc.tensor.matmul(o_bank[n % 4], gated[:, buf * GJ + j, t * P:(t + 1) * P], vrows[:, j, half * HT:(half + 1) * HT],
                                                start=(j == 0), stop=(j == GJ - 1))
                    last.then_inc(o_full, 1)

            tiles_of(0)
            with pe.Fori(0, TURNS) as b:
                for i in range(PER_TURN):
                    tiles_of(b * PER_TURN + i + 1)
                    pieces_of(b * PER_TURN + i, i % GBUFS)
            for i in range(LAST_GROUPS):
                if i < LAST_GROUPS - 1:
                    tiles_of(TURNS * PER_TURN + i + 1)
                pieces_of(TURNS * PER_TURN + i, i % GBUFS)

        @block.scalar
        def _(act):
            act.sem_inc(act_emptied, per_half["act"])
            act.wait_ge(const_in, 80)
            act.wait_ge(const_dve, 3)
            with act.Fori(0, HALVES) as h:
                def full(kind, i):
                    act.wait_ge(pe_step, h * NSTEP + position[kind, i] + 2)
                    return psum[:, position[kind, i] % PAIRS, :]

                act.wait_ge(dve_emptied, h * TT + TT)
                for t in range(2):
                    act.dma_start(xt[:, t, :], x[bass.ds(h * TT + t, 1), :, :].rearrange("o p n -> (o p) n")).then_inc(xt_loaded[t], 16)
                pair = full("sumsq", 0)
                nc.scalar.activation(std[:, 0:COLS].rearrange("p (c t) -> p c t", c=2),
                                     pair.rearrange("p (c t) -> p c t", c=2)[:, :, 0:HB], ACT.Sqrt,
                                     bias=eps, scale=1.0 / D).then_inc(act_emptied, 1)
                for i in range(CT):
                    pair = full("proj", i)
                    nc.scalar.activation(proj[:, i, :].rearrange("p (c t) -> p c t", c=2),
                                         pair.rearrange("p (c t) -> p c t", c=2)[:, :, 0:HB], ACT.Copy).then_inc(act_emptied, 1)
                for i in range(2):
                    pair = full("pool", i)
                    for c in range(2):
                        g = 2 * i + c
                        last = nc.scalar.activation(proj[:, g, 0:HT], pair[:, c * HT:(c + 1) * HT], ACT.Copy, scale=pscale[:, g:g + 1])
                    last.then_inc(act_emptied, 1)
                act.drain()
                for g in range(NG):
                    nc.scalar.activation(xnT[:, g, 0:HT], proj[:, g, 0:HT], ACT.Square)
                for g in range(NG):
                    act.wait_ge(conv_done, h * NG + g + 1)
                    last = nc.scalar.activation(xnT[:, NG + g, 0:HT], proj[:, 12 + g, 0:HT], ACT.Square)
                last.then_inc(squares, 1)
                pair = full("ynorm", 0)
                nc.scalar.activation(std, pair, ACT.Sqrt, bias=eps, scale=1.0 / (NG * P)).then_inc(act_emptied, 1)
                for t in range(TT):
                    act.wait_ge(dve_emptied, (h + 1) * TT + t + 1)
                    nc.scalar.activation(squared, h2b[:, t % 2, :], ACT.Square, accum_out=col[:, 1 + t:2 + t])
                    act.drain()
                    nc.scalar.activation(col[:, 5 + t:6 + t], col[:, 1 + t:2 + t], ACT.Sqrt, bias=eps, scale=1.0 / D).then_inc(std_ready, 1)
                    if t < 2:
                        act.dma_start(xt[:, t, :], x[bass.ds(h * TT + t + 2, 1), :, :].rearrange("o p n -> (o p) n")).then_inc(xt_loaded[t], 16)
                for t in range(TT):
                    pair = full("turn", t)
                    nc.scalar.activation(xnT[:, :, t * P:(t + 1) * P], pair.rearrange("p (k t) -> p k t", k=KD), ACT.Copy).then_inc(act_emptied, 1)
                act.wait_ge(y_ready, h * KD + KD)
                for i in range(CT // 2):
                    pair = full("query", i)
                    nc.scalar.activation(proj[:, 2 * i:2 * i + 2, 0:HT], pair.rearrange("p (c t) -> p c t", c=2), ACT.Copy).then_inc(act_emptied, 1)
                for i in range(2 * TT):
                    pair = full("score", i)
                    if i % 2 == 0 and i > 0:
                        act.wait_ge(scores_kept, h * (16 * TT) + 16 * (i // 2))
                    nc.scalar.activation(scores[:, (i % 2) * D:(i % 2 + 1) * D], pair, ACT.Copy).then_inc(act_emptied, 1)

            act.sem_inc(table_out, 4)
            act.sem_inc(act_ready, GJ)
            act.wait_ge(d_shifted, 1)
            nc.scalar.activation(route[:, 2, :, :], route[:, 2, :, :], ACT.Exp).then_inc(d_exped, 1)
            for t in range(DENSE_TILES):
                act.wait_ge(turned, t + 1)
                nc.scalar.activation(routeT[:, :, t, :], bank[4 + t][:, 0:3 * P].rearrange("p (m k) -> p m k", m=3), ACT.Copy).then_inc(turned_out, 1)
            act.wait_ge(mixers_done, 1)

            def first_hots(batch, c):
                for t in range(HOTS):
                    nc.scalar.activation(hots[:, c, 0, t, :], iota[:], ACT.Square, scale=-1.0,
                                         bias=keysT[:, 0, bass.ds(batch * HOTS + t, 1)])
                act.drain()
                nc.scalar.activation(hots[:, c, 0], hots[:, c, 0], ACT.Relu, scale=-4.0, bias=ones[:, 0:1]).then_inc(hot_first, 1)

            def tables_out(it, first, last):
                batches = 2 * CHUNK // HOTS
                for n in range(CHUNK // 2):
                    if n % 2 == 0 and not (last and n // 2 + 2 >= batches):
                        first_hots(it * batches + n // 2 + 2, (n // 2 + 2) % HOTBUFS)
                    c, m = n // (CHUNK // 4), n % (CHUNK // 4)
                    if m == 0 and not first:
                        act.wait_ge(table_kept[c], it * 16)
                        act.sem_inc(act_go, 1)
                    act.wait_ge(table_full, it * (CHUNK // 2) + n + 2 * HOTBUFS + 1)
                    nc.scalar.activation(tables[:, c, :, 4 * m:4 * m + 4, :].rearrange("p g t j -> p t g j"),
                                         g_bank[n % 4].rearrange("p (t g j) -> p t g j", t=4, g=GROUPS), ACT.Copy).then_inc(table_out, 1)

            act.drain()
            first_hots(0, 0)
            first_hots(1, 1)
            tables_out(0, True, False)
            with act.Fori(1, HT // (2 * CHUNK) - 1) as it:
                tables_out(it, False, False)
            tables_out(HT // (2 * CHUNK) - 1, False, True)

            def gelu_tiles(b, first, count):
                for n in range(first + GJ, first + GJ + count):
                    act.wait_ge(s_full, b * (GJ * PER_TURN) + n + USLOTS + 1)
                    act.wait_ge(w_ready, b * (GJ * PER_TURN) + n + 1)
                    act.sem_inc(act_go, 1)
                    nc.scalar.activation(acts[:, n % GJ, :], s_bank[n % GJ], ACT.Gelu).then_inc(act_ready, 1)

            def gelu_dots(b):
                act.wait_ge(rows_used, b * (2 * HK) + RING + HK)
                nc.scalar.activation(gelu[:], dots[:], ACT.Gelu).then_inc(gelu_done, 1)

            def last_norm(b):
                act.wait_ge(h3_ready, b + 2)
                nc.scalar.activation(acc[:, 1, :], acc[:, 0, :], ACT.Square, accum_out=col[:, 9:10])
                act.drain()
                nc.scalar.activation(col[:, 10:11], col[:, 9:10], ACT.Sqrt, bias=eps, scale=1.0 / D).then_inc(root_done, 1)

            def store(b):
                act.wait_ge(out_ready, b + 1)
                act.sem_inc(act_go, 1)
                act.dma_start(out[bass.ds(b + DENSE_TILES, 1), :, :].rearrange("o p n -> (o p) n"), acc[:, 1, :]).then_inc(out_kept, 16)

            n_out = gated_tiles(turn_items[:turn_spread[HK - 1]])
            act.wait_ge(shifted, 1)
            nc.scalar.activation(gexp[:].rearrange("p h k -> p (h k)"), weight[:], ACT.Exp).then_inc(exped, 1)
            gelu_tiles(0, -GJ, GJ)
            act.wait_ge(dots_kept, HOT_TURNS)
            gelu_dots(0)
            with act.Fori(0, TURNS) as b:
                gelu_tiles(b, 0, n_out)
                last_norm(b)
                act.wait_ge(shifted, b + 2)
                nc.scalar.activation(gexp[:].rearrange("p h k -> p (h k)"), weight[:], ACT.Exp).then_inc(exped, 1)
                store(b)
                gelu_tiles(b, n_out, GJ * PER_TURN - n_out)
                gelu_dots(b + 1)
            gelu_tiles(TURNS, 0, gated_tiles(last_items))
            for t in range(DENSE_TILES):
                act.wait_ge(o_added, 4 + (GROUPS - 1) * SUMS + 2 * t + 2)
                nc.scalar.activation(junk_a, sums[:, t, :], ACT.Square, accum_out=col[:, 1 + t:2 + t])
                act.drain()
                nc.scalar.activation(col[:, 5 + t:6 + t], col[:, 1 + t:2 + t], ACT.Sqrt, bias=eps, scale=1.0 / D).then_inc(root_done, 1)
            last_norm(BLOCKS - 1)
            act.wait_ge(out_ready, TILES)
            act.dma_start(out[TILES - 1, :, :], acc[:, 1, :]).then_inc(out_kept, 16)
            act.wait_ge(out_kept, 16 * TILES)

        @block.vector
        def _(dve):
            nc.vector.memset(ident[:], 1.0).then_inc(const_dve, 1)
            nc.vector.memset(ones[:], 1.0).then_inc(const_dve, 1)
            nc.vector.memset(eps, EPS).then_inc(const_dve, 1)
            dve.sem_inc(dve_emptied, per_half["dve"])
            dve.sem_inc(rows_used, RING)
            dve.sem_inc(s_used, 1)
            dve.sem_inc(h3_ready, 1)
            dve.sem_inc(w_ready, GJ)
            dve.sem_inc(o_added, 4)
            dve.wait_ge(const_in, 80)
            def rank_keys(q):
                four = [(hp, ranking[:, hp * KEYS:(hp + 1) * KEYS], work[:, i * KEYS:(i + 1) * KEYS])
                        for i, hp in enumerate(range(4 * q, 4 * q + 4))]
                for hp, s, _ in four:
                    nc.vector.max(tops[:, hp, 0:8], s)
                dve.drain()
                for hp, s, rest in four:
                    nc.vector.max_index(topi[:, hp, 0:8], tops[:, hp, 0:8], s)
                    nc.vector.match_replace(rest, tops[:, hp, 0:8], s, LOWEST)
                dve.drain()
                for hp, _, rest in four:
                    nc.vector.max(tops[:, hp, 8:16], rest)
                dve.drain()
                for hp, _, rest in four:
                    nc.vector.max_index(topi[:, hp, 8:16], tops[:, hp, 8:16], rest)
                dve.drain()

            def rank_pairs(q):
                n = TOPK * TOPK
                cand, rest, hot = (views["pair_scratch"][:, a * n:b * n] for a, b in ((0, 2), (2, 4), (4, 8)))
                two = [(2 * q + i, cand[:, i * n:(i + 1) * n], rest[:, i * n:(i + 1) * n]) for i in range(2)]
                for hd, c, _ in two:
                    nc.vector.tensor_tensor(c.rearrange("p (a b) -> p a b", a=TOPK),
                                            tops[:, 2 * hd, :].unsqueeze(2).to_broadcast([P, TOPK, TOPK]),
                                            tops[:, 2 * hd + 1, :].unsqueeze(1).to_broadcast([P, TOPK, TOPK]), ALU.add)
                dve.drain()
                for hd, c, _ in two:
                    nc.vector.max(best[:, hd, 0:8], c)
                dve.drain()
                for hd, c, left in two:
                    nc.vector.max_index(pos[:, hd, 0:8], best[:, hd, 0:8], c)
                    nc.vector.match_replace(left, best[:, hd, 0:8], c, LOWEST)
                dve.drain()
                for hd, _, left in two:
                    nc.vector.max(best[:, hd, 8:16], left)
                dve.drain()
                for hd, _, left in two:
                    nc.vector.max_index(pos[:, hd, 8:16], best[:, hd, 8:16], left)
                dve.drain()
                both = pos[:, 2 * q:2 * q + 2, :]
                nc.vector.tensor_scalar(digit[:, :, 0, :], both, 4, None, ALU.logical_shift_right)
                nc.vector.tensor_scalar(digit[:, :, 1, :], both, TOPK - 1, None, ALU.bitwise_and)
                dve.drain()
                hot = hot.rearrange("p (h k a) -> p h k a", h=4, k=TOPK)
                nc.vector.tensor_tensor(hot, digit[:].rearrange("p h s k -> p (h s) k").unsqueeze(3).to_broadcast([P, 4, TOPK, TOPK]),
                                        iota[:, 0:TOPK].unsqueeze(1).unsqueeze(1).to_broadcast([P, 4, TOPK, TOPK]), ALU.is_equal)
                dve.drain()
                nc.vector.tensor_tensor(hot, hot, topi[:, 4 * q:4 * q + 4, :].unsqueeze(2).to_broadcast([P, 4, TOPK, TOPK]), ALU.mult)
                dve.drain()
                nc.vector.tensor_reduce(half_i[:, :, 2 * q * TOPK:(2 * q + 2) * TOPK].rearrange("p s (h k) -> p h s k", h=2),
                                        hot.rearrange("p (h s) k a -> p h s k a", s=2), AX.X, ALU.add)
                dve.drain()

            def keep_dense(t):
                nc.vector.tensor_copy(route[:, 0:2, t, :], half_i[:])
                last = nc.vector.tensor_tensor(route[:, 2, t, :].rearrange("p (h k) -> p h k", h=HEADS), best[:],
                                               best[:, :, 0:1].to_broadcast([P, HEADS, TOPK]), ALU.subtract)
                if t == DENSE_TILES - 1:
                    last.then_inc(d_shifted, 1)
                dve.drain()
                dve.sem_inc(s_used, 1)

            def rank_dense(t):
                dve.wait_ge(s_loaded, 16 * t + 16)
                for q in range(4):
                    rank_keys(q)
                for q in range(4):
                    rank_pairs(q)
                keep_dense(t)

            def mixers(h):
                def act_has(kind, i):
                    _, until = emptied_until(position[kind, i])
                    dve.wait_ge(act_emptied, (h + 1) * per_half["act"] + until)

                if h > 0:
                    dve.wait_ge(pe_step, (h - 1) * NSTEP + position["outp", TT - 1] + 2)
                for k in range(KD):
                    if k % 4 == 0:
                        dve.wait_ge(xT_loaded[k // 4], h * 16 + 16)
                    nc.vector.tensor_tensor(xsq[:, k, :], xnT[:, k, :], xnT[:, k, :], ALU.mult).then_inc(x_squared, 1)
                act_has("sumsq", 0)
                nc.vector.reciprocal(rstd[:, 0:COLS], std[:, 0:COLS])
                dve.drain()
                for k in range(KD):
                    nc.vector.scalar_tensor_tensor(out=xnT[:, k, :], in0=xnT[:, k, :], scalar=g_mix[:, k:k + 1],
                                                   in1=rstd[:, 0:COLS], op0=ALU.mult, op1=ALU.mult).then_inc(xn_ready, 1)
                if h == 1:
                    rank_dense(0)
                for g in range(NG):
                    act_has("proj", g)
                    a = proj[:, g, :]
                    src, width = a, 1
                    for r in range(g + 1):
                        dst = tA if r % 2 == 0 else tB
                        nc.vector.tensor_tensor(dst[:, 2 * width - 1:COLS], src[:, 2 * width - 1:COLS],
                                                src[:, width - 1:COLS - width], ALU.add)
                        dve.drain()
                        src, width = dst, 2 * width
                    nc.vector.scalar_tensor_tensor(out=yT[:, g, :], in0=src[:, META:COLS], scalar=1.0 / width,
                                                   in1=a[:, META:COLS], op0=ALU.mult, op1=ALU.subtract).then_inc(pooled, 1)
                    dve.drain()
                if h == 1:
                    dve.wait_ge(s_loaded, 32)
                    for q in range(4):
                        rank_keys(q)
                for g in range(NG):
                    act_has("proj", 12 + g)
                    b_gate, c_gate, val = (proj[:, 4 * q + g, :] for q in (1, 2, 3))
                    nc.vector.tensor_tensor(c_gate, c_gate, val, ALU.mult)
                    dve.drain()
                    nc.vector.tensor_scalar(tA[:, META:COLS], c_gate[:, META - 2:COLS - 2], convw[:, 0, g:g + 1], None, ALU.mult)
                    dve.drain()
                    nc.vector.scalar_tensor_tensor(out=tB[:, META:COLS], in0=c_gate[:, META - 1:COLS - 1], scalar=convw[:, 1, g:g + 1],
                                                   in1=tA[:, META:COLS], op0=ALU.mult, op1=ALU.add)
                    dve.drain()
                    nc.vector.scalar_tensor_tensor(out=tA[:, META:COLS], in0=c_gate[:, META:COLS], scalar=convw[:, 2, g:g + 1],
                                                   in1=tB[:, META:COLS], op0=ALU.mult, op1=ALU.add)
                    dve.drain()
                    nc.vector.tensor_tensor(val[:, 0:HT], b_gate[:, META:COLS], tA[:, META:COLS], ALU.mult).then_inc(conv_done, 1)
                act_has("ynorm", 0)
                nc.vector.reciprocal(rstd, std)
                dve.drain()
                for k in range(KD):
                    src = proj[:, k if k < NG else 8 + k, 0:HT]
                    r = rstd[:, 0:HT] if k < NG else rstd[:, HT:2 * HT]
                    nc.vector.scalar_tensor_tensor(out=yT[:, k, :], in0=src, scalar=g_ab[:, k:k + 1], in1=r,
                                                   op0=ALU.mult, op1=ALU.mult).then_inc(y_ready, 1)
                for t in range(TT):
                    n = position["outp", t]
                    dve.wait_ge(pe_step, h * NSTEP + n + 2)
                    dve.wait_ge(xt_loaded[t % 2], h * 32 + 16 * (t // 2) + 16)
                    if t >= 2:
                        dve.wait_ge(kept[t % 2], h * 64 + 32 * (t // 2))
                    nc.vector.tensor_tensor(h2b[:, t % 2, :], psum[:, n % PAIRS, :], xt[:, t % 2, :], ALU.add).then_inc(dve_emptied, 1)
                    dve.wait_ge(std_ready, h * TT + t + 1)
                    nc.vector.reciprocal(col[:, 11 + t % 2:12 + t % 2], col[:, 5 + t:6 + t])
                    dve.drain()
                    if t >= 2:
                        dve.wait_ge(pe_step, h * NSTEP + position["turn", t - 2] + 2)
                    nc.vector.scalar_tensor_tensor(out=xfb[:, t % 2, :], in0=h2b[:, t % 2, :], scalar=col[:, 11 + t % 2:12 + t % 2],
                                                   in1=g_ffn, op0=ALU.mult, op1=ALU.mult).then_inc(xf_ready, 1)
                    if h == 1:
                        rank_pairs(t)
                if h == 1:
                    for t in range(1, DENSE_TILES):
                        keep_dense(t) if t == 1 else rank_dense(t)

            for h in range(HALVES):
                mixers(h)

            dve.wait_ge(s_loaded, 16 * (DENSE_TILES + 1))
            for q in range(2):
                rank_keys(q)
                rank_pairs(q)
            scores_d = route[:, 2, :, :].rearrange("p t (h k) -> p (t h) k", h=HEADS)
            dve.wait_ge(d_exped, 1)
            nc.vector.tensor_reduce(gsum[:, 0, :], scores_d, AX.X, ALU.add)
            dve.drain()
            nc.vector.reciprocal(gsum[:, 1, :], gsum[:, 0, :])
            dve.drain()
            nc.vector.tensor_tensor(scores_d, scores_d, gsum[:, 1, :].unsqueeze(2).to_broadcast([P, DENSE_TILES * HEADS, TOPK]),
                                    ALU.mult).then_inc(d_gates, 1)

            def experts_of(idx, first=0, end=HK):
                return nc.vector.scalar_tensor_tensor(out=idx[:, first:end], in0=half_i[:, 0, first:end], scalar=float(KEYS),
                                                      in1=half_i[:, 1, first:end], op0=ALU.mult, op1=ALU.add)

            def hand_over():
                nc.vector.tensor_tensor(weight[:].rearrange("p (h k) -> p h k", h=HEADS), best[:],
                                        best[:, :, 0:1].to_broadcast([P, HEADS, TOPK]), ALU.subtract).then_inc(shifted, 1)
                experts_of(idx_v).then_inc(routed_v, 1)
                dve.drain()
                dve.sem_inc(s_used, 1)

            def normalise(b):
                dve.wait_ge(exped, b + 1)
                nc.vector.tensor_reduce(gsum[:, 0, 0:HEADS], gexp[:], AX.X, ALU.add)
                dve.drain()
                nc.vector.reciprocal(gsum[:, 1, 0:HEADS], gsum[:, 0, 0:HEADS])
                dve.drain()
                nc.vector.tensor_tensor(gates[:].rearrange("p (h k) -> p h k", h=HEADS), gexp[:],
                                        gsum[:, 1, 0:HEADS].unsqueeze(2).to_broadcast([P, HEADS, TOPK]), ALU.mult)
                dve.drain()

            def dense_item(b, kind, i, m):
                if kind == "gate":
                    if m == 0:
                        dve.wait_ge(g_in, b * (16 * PER_TURN) + 16 * i + 16)
                    dve.wait_ge(act_ready, b * (GJ * PER_TURN) + i * GJ + m + GJ + 1)
                    nc.vector.tensor_tensor(gated[:, (i % GBUFS) * GJ + m, :], acts[:, m, :],
                                            gtab.rearrange("p (t j) -> p t j", j=GJ)[:, :, m], ALU.mult).then_inc(w_ready, 1)
                else:
                    dve.wait_ge(o_full, b * (SUMS * PER_TURN) + i * SUMS + m + 2)
                    piece = sums[:, m // 2, (m % 2) * HT:(m % 2 + 1) * HT]
                    nc.vector.tensor_tensor(piece, piece, o_bank[m % 4], ALU.add).then_inc(o_added, 1)

            RANK_AT = [HK * (q + 1) // 5 for q in range(4)]

            def row_ready(r, cycle, slot):
                dve.wait_ge(row_in[slot], cycle * 16 + 16)
                dve.wait_ge(rows_used, r + RING - 1)

            def dot(to, slot):
                nc.vector.tensor_tensor_reduce(out=junk[:, slot % 2, :], in0=ring[:, slot, :], in1=xf, scale=1.0, scalar=0.0,
                                               op0=ALU.mult, op1=ALU.add, accum_out=to).then_inc(rows_used, 1)

            def weigh(k):
                row = ring[:, k % RING, :]
                if k < 2:
                    nc.vector.tensor_scalar(acc[:, k, :], row, weight[:, k:k + 1], None, ALU.mult).then_inc(rows_used, 1)
                else:
                    nc.vector.scalar_tensor_tensor(out=acc[:, k % 2, :], in0=row, scalar=weight[:, k:k + 1], in1=acc[:, k % 2, :],
                                                   op0=ALU.mult, op1=ALU.add).then_inc(rows_used, 1)

            def output_rows(b, items, done_after, rank_next):
                dve.wait_ge(gelu_done, b + 1)
                nc.vector.tensor_tensor(weight[:], gelu[:], gates[:], ALU.mult)
                dve.drain()
                done = 0
                for n in range(HK):
                    row_ready(b * (2 * HK) + HK + n, b * (2 * HK // RING) + (HK + n) // RING, n % RING)
                    weigh(n)
                    for item in items[done:done_after[n]]:
                        dense_item(b, *item)
                    done = done_after[n]
                    if not rank_next and n >= HK - RING and n % 2 == 1:
                        t = (n - (HK - RING)) // 2
                        dve.wait_ge(root_done, BLOCKS + t)
                        nc.vector.reciprocal(col[:, 5 + t:6 + t], col[:, 5 + t:6 + t])
                        dve.drain()
                        nc.vector.scalar_tensor_tensor(out=sums[:, t, :], in0=sums[:, t, :], scalar=col[:, 5 + t:6 + t], in1=g_final[:],
                                                       op0=ALU.mult, op1=ALU.mult).then_inc(out_ready, 1)
                    if rank_next and n in RANK_AT:
                        rank_pairs(RANK_AT.index(n))
                        if n == RANK_AT[-1]:
                            experts_of(idx_u).then_inc(routed_u, 1)
                dve.drain()
                nc.vector.tensor_tensor(acc[:, 0, :], acc[:, 0, :], acc[:, 1, :], ALU.add)
                dve.drain()
                dve.wait_ge(h2_in, b * 16 + 16)
                nc.vector.tensor_tensor(acc[:, 0, :], acc[:, 0, :], h2, ALU.add).then_inc(h3_ready, 1)
                if rank_next:
                    hand_over()

            def finish(roots):
                dve.wait_ge(root_done, roots)
                nc.vector.reciprocal(col[:, 13:14], col[:, 10:11])
                dve.drain()
                nc.vector.scalar_tensor_tensor(out=acc[:, 1, :], in0=acc[:, 0, :], scalar=col[:, 13:14], in1=g_final[:],
                                               op0=ALU.mult, op1=ALU.mult).then_inc(out_ready, 1)

            def turn(b, rank_after):
                output_rows(b, turn_items, turn_spread, True)
                done = turn_spread[HK - 1]
                dve.wait_ge(xf_in, b * 16 + 32)
                for n in range(HK):
                    row_ready(b * (2 * HK) + 2 * HK + n, b * (2 * HK // RING) + (2 * HK + n) // RING, n % RING)
                    dot(dots[:, n:n + 1], n % RING)
                    if n == RING // 2:
                        finish(b + 1)
                    if rank_after and n in RANK_AT:
                        if n == RANK_AT[0]:
                            dve.wait_ge(s_loaded, b * 16 + 16 * (DENSE_TILES + 3))
                            dve.sem_inc(dve_go, 1)
                        rank_keys(RANK_AT.index(n))
                    for item in turn_items[done:turn_spread[HK + n]]:
                        dense_item(b, *item)
                    done = turn_spread[HK + n]
                normalise(b + 1)
                dve.wait_ge(out_kept, b * 16 + 16)

            dve.wait_ge(mixers_done, 1)
            experts_of(idx_u, 0, HK // 2).then_inc(routed_u, 1)

            def second_hots(it, c):
                dve.wait_ge(table_full, it * (2 * HOTBUFS) + 2 * c + 2)
                dve.sem_inc(dve_go, 1)
                nc.vector.tensor_tensor(hots[:, c, 1], iota[:].unsqueeze(1).to_broadcast([P, HOTS, KEYS]),
                                        keysT[:, 1, bass.ds((it * HOTBUFS + c) * HOTS, HOTS)].unsqueeze(2).to_broadcast([P, HOTS, KEYS]),
                                        ALU.is_equal).then_inc(hot_ready, 1)

            dve.wait_ge(turned_out, DENSE_TILES)
            dve.wait_ge(xf_in, 16)

            def first_rows(it, c):
                for i in range(HOT_ROWS):
                    slot = c * HOT_ROWS + i
                    row_ready(it * RING + slot, it, slot)
                    dot(dots_now[:, slot:slot + 1], slot)
                if c == HOTBUFS - 1:
                    dve.drain()
                    nc.vector.tensor_copy(dots[:, bass.ds(it * RING, RING)], dots_now[:]).then_inc(dots_kept, 1)
                    dve.drain()

            for it in range(RANK_TURNS):
                for c in range(HOTBUFS):
                    second_hots(it, c)
                    first_rows(it, c)
                    n = it * HOTBUFS + c
                    if n in (1, 4):
                        rank_keys(2 + n // 3)
                    if n in (3, 6):
                        rank_pairs(1 + n // 3)
                    if n == 6:
                        experts_of(idx_u, HK // 2, HK).then_inc(routed_u, 1)
                        hand_over()
            with dve.Fori(RANK_TURNS, HOT_TURNS) as it:
                for c in range(HOTBUFS):
                    second_hots(it, c)
                    first_rows(it, c)
            dve.wait_ge(s_loaded, 16 * (DENSE_TILES + 2))
            for q in range(GJ):
                rank_keys(q)
                dense_item(0, "gate", 0, q)
            normalise(0)
            dve.wait_ge(d_h2_in, 16)
            with dve.Fori(0, TURNS - 1) as b:
                turn(b, True)
            turn(TURNS - 1, False)
            output_rows(BLOCKS - 1, last_items, last_spread, False)
            finish(TILES)


def kernel(x, meta_tokens, norm_mix_g, w_in, pool_w, pool_scale, conv_w, norm_a_g, norm_b_g, w_out, norm_ffn_g,
           w_query, sub_keys, expert_u, expert_v, norm_final_g):
    import concourse.bacc as bacc
    from concourse.bass_utils import run_bass_kernel_spmd

    a = lambda v: np.asarray(v)
    tiles_first = lambda w: np.ascontiguousarray(w.reshape(KD, P, -1).transpose(1, 0, 2))
    per_partition = lambda v: v.reshape(-1, P).T
    x2 = a(x)[0]
    h = np.concatenate([a(meta_tokens), x2], axis=0)
    small = np.concatenate([per_partition(a(norm_mix_g)[0]), per_partition(a(pool_scale)[0]),
                            per_partition(a(conv_w)[0].reshape(-1)), per_partition(a(norm_a_g)[0]),
                            per_partition(a(norm_b_g)[0])], axis=1)
    rows_g = np.concatenate([a(norm_ffn_g)[0], a(norm_final_g)])[None, :].repeat(P, axis=0)
    arrays = {
        "hT": tiles_first(h.T),
        "x": x2.reshape(TILES, P, D),
        "w_in": tiles_first(a(w_in)[0]),
        "w_out": tiles_first(a(w_out)[0]),
        "w_query": tiles_first(a(w_query)[0]),
        "sub_keys": a(sub_keys)[0].transpose(3, 0, 1, 2).reshape(P, HP * KEYS),
        "pool_w": a(pool_w)[0].transpose(1, 0, 2).reshape(P, NG * P),
        "small": small,
        "rows_g": rows_g,
        "expert_u": a(expert_u)[0],
        "expert_v": a(expert_v)[0],
        "uT": a(expert_u)[0].reshape(KEYS, KEYS, KD, P).transpose(1, 3, 2, 0).reshape(KEYS, P, D),
    }
    arrays = {f"in_{n}": np.ascontiguousarray(v) for n, v in arrays.items()}
    nc = bacc.Bacc("TRN2", target_bir_lowering=False, num_devices=1)
    args = [nc.dram_tensor(n, v.shape, mybir.dt.from_np(v.dtype), kind="ExternalInput").ap() for n, v in arrays.items()]
    result = nc.dram_tensor("out", (TILES, P, D), FP32, kind="ExternalOutput").ap()
    program(nc, *args, result)
    r = run_bass_kernel_spmd(nc, [arrays], core_ids=[0])
    return r.results[0]["out"].reshape(1, SEQ, D)
```
